# Optimizing a Trainium2 kernel written in Bass

```python
import jax, jax.numpy as jnp
from jax import lax
import numpy as np
import math
import jax
import jax.numpy as jnp

D_MODEL = 1024
BATCH = 1
SEQ = 512
DEPTH = 1

N_META = 16
CONV_WIDTH = D_MODEL
CONV_KERNEL = 31
RWKV_HEAD = 64
RWKV_HEADS = D_MODEL // RWKV_HEAD
RWKV_WIDTH = RWKV_HEADS * RWKV_HEAD
DECAY_LORA = 64
ICLR_LORA = 64
GATE_LORA = 160
D_FF = 2816
FFN_KERNEL = 3
ALPHA = (2.0 * DEPTH) ** 0.25
BETA = (8.0 * DEPTH) ** -0.25
LN_EPS = 1e-5
GN_EPS = 64e-5

N_RWKV_COLS = 3 * RWKV_WIDTH + DECAY_LORA + ICLR_LORA + GATE_LORA
N_IN = 2 * CONV_WIDTH + N_RWKV_COLS + 2 * D_MODEL


def layer_norm(x, g, b, eps=LN_EPS):
    xf = x.astype(jnp.float32)
    mu = jnp.mean(xf, axis=-1, keepdims=True)
    xc = xf - mu
    var = jnp.mean(xc * xc, axis=-1, keepdims=True)
    y = xc * lax.rsqrt(var + eps) * g.astype(jnp.float32) + b.astype(jnp.float32)
    return y.astype(x.dtype)

def causal_dwconv(x, w):
    k, c = w.shape
    return lax.conv_general_dilated(
        x, w[:, None, :].astype(x.dtype), window_strides=(1,), padding=[(k - 1, 0)],
        dimension_numbers=("NWC", "WIO", "NWC"), feature_group_count=c)

def token_shift(p):
    return jnp.pad(p, ((0, 0), (1, 0), (0, 0)))[:, :-1]

def rwkv7_recurrence(r, decay, k, v, a, b):
    bsz, _, h, n = r.shape

    def step(s, inp):
        r_t, w_t, k_t, v_t, a_t, b_t = inp
        sa = jnp.einsum("bhvk,bhk->bhv", s, a_t)
        s = s * w_t[:, :, None, :] + sa[..., None] * b_t[:, :, None, :] + v_t[..., None] * k_t[:, :, None, :]
        y = jnp.einsum("bhvk,bhk->bhv", s, r_t)
        return s, y

    xs = tuple(jnp.moveaxis(z, 1, 0) for z in (r, decay, k, v, a, b))
    s0 = jnp.zeros((bsz, h, n, n), jnp.float32)
    _, ys = lax.scan(step, s0, xs)
    return jnp.moveaxis(ys, 0, 1)

def rwkv7_time_mix(p, mu, w0, w_decay_up, a0, a_up, g_up, k_k, k_a, r_k, lnx_g, lnx_b, w_out):
    bsz, t, _ = p.shape
    h, n, wd = RWKV_HEADS, RWKV_HEAD, RWKV_WIDTH
    p = p + (token_shift(p) - p) * mu
    i1, i2, i3 = wd, 2 * wd, 3 * wd
    i4, i5 = i3 + DECAY_LORA, i3 + DECAY_LORA + ICLR_LORA
    r, k, v = p[..., :i1], p[..., i1:i2], p[..., i2:i3]
    xw, xa, xg = p[..., i3:i4], p[..., i4:i5], p[..., i5:]
    w = -jax.nn.softplus(-(w0 + jnp.tanh(xw) @ w_decay_up)) - 0.5
    a = jax.nn.sigmoid(a0 + xa @ a_up)
    g = jax.nn.sigmoid(xg) @ g_up
    heads = lambda z: z.reshape(bsz, t, h, n).astype(jnp.float32)
    kk = heads(k * k_k)
    kk = kk / jnp.maximum(jnp.sqrt(jnp.sum(kk * kk, axis=-1, keepdims=True)), 1e-12)
    k = k * (1.0 + (a - 1.0) * k_a)
    decay = jnp.exp(-jnp.exp(heads(w)))
    rh, kh, vh, ah = heads(r), heads(k), heads(v), heads(a)
    o = rwkv7_recurrence(rh, decay, kh, vh, -kk, kk * ah)
    o = layer_norm(o, lnx_g.reshape(h, n), lnx_b.reshape(h, n), GN_EPS)
    o = o + jnp.sum(rh * kh * r_k.astype(jnp.float32), axis=-1, keepdims=True) * vh
    o = o.reshape(bsz, t, wd).astype(p.dtype) * g
    return o @ w_out

def conformer_conv(p, conv_dw, conv_dw_b, conv_ln_g, conv_ln_b, w_conv_out):
    c = p[..., :CONV_WIDTH] * jax.nn.sigmoid(p[..., CONV_WIDTH:])
    c = causal_dwconv(c, conv_dw) + conv_dw_b
    c = jax.nn.silu(layer_norm(c, conv_ln_g, conv_ln_b))
    return c @ w_conv_out

def conv_gated_mlp(h, ffn_up, ffn_dw, ffn_down):
    u = causal_dwconv(h @ ffn_up, ffn_dw)
    return (jax.nn.silu(u[..., D_FF:]) * u[..., :D_FF]) @ ffn_down

def first_inputs(seed: int = 0) -> dict:
    key = jax.random.key(seed)
    ks = iter(jax.random.split(key, 40))
    L, D = DEPTH, D_MODEL

    def nrm(shape, scale):
        return scale * jax.random.normal(next(ks), shape, jnp.float32)

    def gain(shape):
        return 1.0 + nrm(shape, 0.02)

    def unif(shape, lo, hi):
        return jax.random.uniform(next(ks), shape, jnp.float32, minval=lo, maxval=hi)

    return {
        "x": nrm((BATCH, SEQ, D), 1.0),
        "meta_tokens": nrm((N_META, D), 1.0),
        "ln_in_g": gain((D,)),
        "ln_in_b": nrm((D,), 0.02),
        "w_in": nrm((L, D, N_IN), D ** -0.5),
        "b_gate": nrm((L, 2 * D), 0.02),
        "conv_dw": nrm((L, CONV_KERNEL, CONV_WIDTH), CONV_KERNEL ** -0.5),
        "conv_dw_b": nrm((L, CONV_WIDTH), 0.02),
        "conv_ln_g": gain((L, CONV_WIDTH)),
        "conv_ln_b": nrm((L, CONV_WIDTH), 0.02),
        "w_conv_out": nrm((L, CONV_WIDTH, D), CONV_WIDTH ** -0.5),
        "rwkv_mu": unif((L, N_RWKV_COLS), 0.1, 0.9),
        "w0": unif((L, RWKV_WIDTH), -6.5, -1.5),
        "w_decay_up": nrm((L, DECAY_LORA, RWKV_WIDTH), 0.1 * DECAY_LORA ** -0.5),
        "a0": nrm((L, RWKV_WIDTH), 0.1),
        "a_up": nrm((L, ICLR_LORA, RWKV_WIDTH), 0.1 * ICLR_LORA ** -0.5),
        "g_up": nrm((L, GATE_LORA, RWKV_WIDTH), GATE_LORA ** -0.5),
        "k_k": 0.85 + nrm((L, RWKV_WIDTH), 0.02),
        "k_a": gain((L, RWKV_WIDTH)),
        "r_k": -0.04 + nrm((L, RWKV_HEADS, RWKV_HEAD), 0.02),
        "lnx_g": gain((L, RWKV_WIDTH)),
        "lnx_b": nrm((L, RWKV_WIDTH), 0.02),
        "w_rwkv_out": nrm((L, RWKV_WIDTH, D), RWKV_WIDTH ** -0.5),
        "w_o": nrm((L, D, D), BETA * D ** -0.5),
        "ln1_g": gain((L, D)),
        "ln1_b": nrm((L, D), 0.02),
        "ffn_up": nrm((L, D, 2 * D_FF), D ** -0.5),
        "ffn_dw": nrm((L, FFN_KERNEL, 2 * D_FF), FFN_KERNEL ** -0.5),
        "ffn_down": nrm((L, D_FF, D), BETA * D_FF ** -0.5),
        "ln2_g": gain((L, D)),
        "ln2_b": nrm((L, D), 0.02),
    }

def first_block(x, meta_tokens, ln_in_g, ln_in_b, w_in, b_gate, conv_dw, conv_dw_b, conv_ln_g,
              conv_ln_b, w_conv_out, rwkv_mu, w0, w_decay_up, a0, a_up, g_up, k_k, k_a, r_k,
              lnx_g, lnx_b, w_rwkv_out, w_o, ln1_g, ln1_b, ffn_up, ffn_dw, ffn_down, ln2_g, ln2_b):
    bsz = x.shape[0]
    meta = jnp.broadcast_to(meta_tokens[None].astype(x.dtype), (bsz, N_META, D_MODEL))
    h = layer_norm(jnp.concatenate([meta, x], axis=1), ln_in_g, ln_in_b)
    c_end = 2 * CONV_WIDTH
    r_end = c_end + N_RWKV_COLS
    for l in range(DEPTH):
        p = h @ w_in[l]
        y_conv = conformer_conv(p[..., :c_end], conv_dw[l], conv_dw_b[l], conv_ln_g[l],
                                conv_ln_b[l], w_conv_out[l])
        y_rwkv = rwkv7_time_mix(p[..., c_end:r_end], rwkv_mu[l], w0[l], w_decay_up[l], a0[l],
                                a_up[l], g_up[l], k_k[l], k_a[l], r_k[l], lnx_g[l], lnx_b[l],
                                w_rwkv_out[l])
        gates = jax.nn.sigmoid(p[..., r_end:] + b_gate[l])
        y = gates[..., :D_MODEL] * y_conv + gates[..., D_MODEL:] * y_rwkv
        h = layer_norm(ALPHA * h + y @ w_o[l], ln1_g[l], ln1_b[l])
        h = layer_norm(ALPHA * h + conv_gated_mlp(h, ffn_up[l], ffn_dw[l], ffn_down[l]),
                       ln2_g[l], ln2_b[l])
    return h[:, N_META:]


_first_inputs = first_inputs


def first_inputs(seed=0):
    import zlib

    import numpy as np

    out = dict(_first_inputs(seed))
    spreads = {}
    factors = {'ln_in_b': 2.74,
     'b_gate': 8.0,
     'conv_dw_b': 8.0,
     'conv_ln_g': 8.0,
     'conv_ln_b': 8.0,
     'w_decay_up': 8.0,
     'a0': 8.0,
     'a_up': 8.0,
     'k_k': 8.0,
     'k_a': 8.0,
     'r_k': 8.0,
     'lnx_g': 8.0,
     'lnx_b': 8.0,
     'ln1_g': 2.737,
     'ln1_b': 2.693,
     'ln2_g': 2.933,
     'ln2_b': 2.769}
    for name, (base, spread) in spreads.items():
        noise = np.random.default_rng([zlib.crc32(name.encode()), seed]).standard_normal(out[name].shape)
        drawn = base * np.exp(spread * noise) if base else spread * noise
        out[name] = __import__('jax').numpy.asarray(drawn.astype(out[name].dtype))
    for name, factor in factors.items():
        out[name] = (out[name] * factor).astype(out[name].dtype)
    return out


_narrow_inputs = first_inputs


def first_inputs(seed=0):

    out = dict(_narrow_inputs(seed))
    wider = {'conv_ln_g': 3.93,
     'conv_ln_b': 3.71,
     'k_k': 6.05,
     'k_a': 3.91,
     'lnx_g': 5.37,
     'lnx_b': 5.09,
     'ln2_g': 3.28,
     'ln2_b': 3.3}
    for name, times in wider.items():
        mean = out[name].mean()
        out[name] = (mean + times * (out[name] - mean)).astype(out[name].dtype)
    return out


DEPTH_2 = 2

GRID_W = 64
CTX_LEN = 256
BRANCH_W = 512
NA_HEADS = 8
NA_DH = BRANCH_W // NA_HEADS
NA_WIN_R = 8
NA_WIN_C = 16
DA_HEADS = 4
DA_DH = 64
DA_VD = 2 * DA_DH
DA_QK = DA_HEADS * 2 * DA_DH
GM_GROUPS = 4
GM_CHUNK = 128
GM_GW = BRANCH_W // GM_GROUPS
N_BRANCH = 3
N_EXPERTS = 16
EC_CAPACITY = 2
EXPERT_FF = 1024
Q_BLOCK = 128
ROPE_THETA = 10000.0
ROPE_AXIS = DA_DH // 2
N_MOD = 6
EPS = 1e-6
KV_SIZES = (BRANCH_W, BRANCH_W, DA_QK, DA_HEADS * DA_VD)
Q_SIZES = (BRANCH_W, DA_QK, BRANCH_W, BRANCH_W, N_BRANCH * D_MODEL)
KV_COLS = sum(KV_SIZES)
PROJ_COLS = KV_COLS + sum(Q_SIZES)


def _split(z, sizes):
    offs = np.cumsum(sizes)[:-1].tolist()
    return jnp.split(z, offs, axis=-1)

def rmsnorm(x, g):
    xf = x.astype(jnp.float32)
    y = xf * lax.rsqrt(jnp.mean(xf * xf, axis=-1, keepdims=True) + EPS)
    return y.astype(x.dtype) * g

def layernorm(x, g, b):
    xf = x.astype(jnp.float32)
    mu = jnp.mean(xf, axis=-1, keepdims=True)
    var = jnp.mean(jnp.square(xf - mu), axis=-1, keepdims=True)
    return ((xf - mu) * lax.rsqrt(var + EPS)).astype(x.dtype) * g + b

def modulate(h, shift, scale):
    return h * (1 + scale) + shift

def rope_tables(n):
    t = jnp.arange(n)
    inv = ROPE_THETA ** (-jnp.arange(0, ROPE_AXIS, 2, dtype=jnp.float32) / ROPE_AXIS)
    ang_r = (t // GRID_W).astype(jnp.float32)[:, None] * inv
    ang_c = (t % GRID_W).astype(jnp.float32)[:, None] * inv
    return (jnp.cos(ang_r), jnp.sin(ang_r), jnp.cos(ang_c), jnp.sin(ang_c))

def _rot(x, cos, sin):
    x1, x2 = jnp.split(x, 2, axis=-1)
    return jnp.concatenate([x1 * cos - x2 * sin, x1 * sin + x2 * cos], axis=-1)

def rope_2d(x, tabs):
    cr, sr, cc, sc = [t.astype(x.dtype)[None, :, None, None, :] for t in tabs]
    xr, xcol = jnp.split(x, 2, axis=-1)
    return jnp.concatenate([_rot(xr, cr, sr), _rot(xcol, cc, sc)], axis=-1)

def dense_attn(q, k, v):
    B, n, H, dh = q.shape
    s = jnp.einsum('bqhd,bkhd->bhqk', q, k) * (dh ** -0.5)
    p = jax.nn.softmax(s.astype(jnp.float32), axis=-1).astype(v.dtype)
    return jnp.einsum('bhqk,bkhd->bqhd', p, v).reshape(B, n, H * dh)

def neighbourhood_attn(q, k, v, kc, vc, rpb):
    B, L, H, dh = q.shape
    Lc = kc.shape[1]
    rows = L // GRID_W
    wr = min(NA_WIN_R, rows)
    scale = dh ** -0.5
    kg = k.reshape(B, rows, GRID_W, H, dh)
    vg = v.reshape(B, rows, GRID_W, H, dh)
    qg = jnp.moveaxis(q.reshape(B, rows, GRID_W, H, dh), 1, 0)
    col = jnp.arange(GRID_W)
    col_start = jnp.clip(col - NA_WIN_C // 2, 0, GRID_W - NA_WIN_C)
    col_idx = col_start[:, None] + jnp.arange(NA_WIN_C)[None, :]
    dc = col_idx - col[:, None] + (NA_WIN_C - 1)

    def row_block(args):
        r, qr = args
        r0 = jnp.clip(r - wr // 2, 0, rows - wr)
        kw = lax.dynamic_slice_in_dim(kg, r0, wr, axis=1)[:, :, col_idx]
        vw = lax.dynamic_slice_in_dim(vg, r0, wr, axis=1)[:, :, col_idx]
        dr = r0 + jnp.arange(wr) - r + (NA_WIN_R - 1)
        bias = jnp.transpose(rpb[:, dr[:, None, None], dc[None]], (0, 2, 1, 3))
        s_loc = jnp.einsum('bqhd,brqjhd->bhqrj', qr, kw) * scale + bias[None]
        s_ctx = jnp.einsum('bqhd,bchd->bhqc', qr, kc) * scale
        s = jnp.concatenate([s_ctx, s_loc.reshape(B, H, GRID_W, wr * NA_WIN_C)], axis=-1)
        p = jax.nn.softmax(s.astype(jnp.float32), axis=-1).astype(v.dtype)
        p_loc = p[..., Lc:].reshape(B, H, GRID_W, wr, NA_WIN_C)
        return (jnp.einsum('bhqc,bchd->bqhd', p[..., :Lc], vc)
                + jnp.einsum('bhqrj,brqjhd->bqhd', p_loc, vw))

    out = lax.map(row_block, (jnp.arange(rows), qg))
    return jnp.moveaxis(out, 0, 1).reshape(B, L, H * dh)

def diff_attend(q, k, v, lam):
    s = jnp.einsum('bqhcd,bkhcd->bhcqk', q, k) * (q.shape[-1] ** -0.5)
    p = jax.nn.softmax(s.astype(jnp.float32), axis=-1)
    a = (p[:, :, 0] - lam * p[:, :, 1]).astype(v.dtype)
    return jnp.einsum('bhqk,bkhd->bqhd', a, v)

def diff_attn_blocks(q, k, v, lam):
    B, L, H, _, dh = q.shape
    nb = L // Q_BLOCK
    qblk = jnp.moveaxis(q.reshape(B, nb, Q_BLOCK, H, 2, dh), 1, 0)
    out = lax.map(lambda qb: diff_attend(qb, k, v, lam), qblk)
    return jnp.moveaxis(out, 0, 1).reshape(B, L, H, v.shape[-1])

def diff_head_norm(o, g, lam_init):
    B, n = o.shape[:2]
    return (rmsnorm(o, g) * (1.0 - lam_init)).reshape(B, n, -1)

def gmlp_gate(u, v, ln_g, ln_b, w_s, b_s):
    B, n, _ = u.shape
    vn = layernorm(v, ln_g, ln_b).reshape(B, n // GM_CHUNK, GM_CHUNK, GM_GROUPS, GM_GW)
    mixed = jnp.einsum('gpq,bnqgc->bnpgc', w_s, vn) + jnp.swapaxes(b_s, 0, 1)[:, :, None]
    return u * mixed.reshape(B, n, BRANCH_W)

def branch_merge(ya, yb, yc, gates, w_branch, w_out):
    ga, gb, gc = jnp.split(jax.nn.sigmoid(gates), N_BRANCH, axis=-1)
    m = ga * (ya @ w_branch[0]) + gb * (yb @ w_branch[1]) + gc * (yc @ w_branch[2])
    return m @ w_out

def ec_moe(h, w_r, w1, w3, w2):
    B, n, D = h.shape
    cap = max(1, EC_CAPACITY * n // N_EXPERTS)
    aff = jax.nn.softmax((h @ w_r).astype(jnp.float32), axis=-1)
    gate, idx = lax.top_k(jnp.swapaxes(aff, 1, 2), cap)
    xin = jax.vmap(lambda hb, ib: hb[ib])(h, idx)
    hid = jax.nn.silu(jnp.einsum('becd,edf->becf', xin, w1)) * jnp.einsum('becd,edf->becf', xin, w3)
    ye = jnp.einsum('becf,efd->becd', hid, w2) * gate[..., None].astype(h.dtype)
    return jax.vmap(lambda yb, ib: jnp.zeros((n, D), h.dtype).at[ib.reshape(-1)].add(yb.reshape(-1, D)))(ye, idx)

def _na_heads(t):
    return t.reshape(t.shape[0], t.shape[1], NA_HEADS, NA_DH)

def _da_qk(t):
    return t.reshape(t.shape[0], t.shape[1], DA_HEADS, 2, DA_DH)

def _da_v(t):
    return t.reshape(t.shape[0], t.shape[1], DA_HEADS, DA_VD)

def second_inputs(seed: int = 0) -> dict:
    key = jax.random.key(seed)
    ks = jax.random.split(key, 32)
    f32 = jnp.float32

    def nrm(k, shape, scale):
        return jax.random.normal(k, shape, f32) * scale

    D = D_MODEL
    return {
        "x": nrm(ks[0], (BATCH, SEQ, D), 1.0),
        "c": nrm(ks[1], (BATCH, D), 1.0),
        "ctx": nrm(ks[2], (BATCH, CTX_LEN, D), 1.0),
        "c_ctx": nrm(ks[3], (D,), 1.0),
        "w_ada": nrm(ks[4], (DEPTH_2, D, N_MOD * D), 0.5 * D ** -0.5),
        "b_ada": nrm(ks[5], (DEPTH_2, N_MOD * D), 0.02),
        "g_norm1": 1.0 + nrm(ks[6], (DEPTH_2, D), 0.05),
        "g_norm2": 1.0 + nrm(ks[7], (DEPTH_2, D), 0.05),
        "w_in": nrm(ks[8], (DEPTH_2, D, PROJ_COLS), D ** -0.5),
        "na_rpb": nrm(ks[9], (DEPTH_2, NA_HEADS, 2 * NA_WIN_R - 1, 2 * NA_WIN_C - 1), 0.1),
        "da_lam_q1": nrm(ks[10], (DEPTH_2, DA_DH), 0.1),
        "da_lam_k1": nrm(ks[11], (DEPTH_2, DA_DH), 0.1),
        "da_lam_q2": nrm(ks[12], (DEPTH_2, DA_DH), 0.1),
        "da_lam_k2": nrm(ks[13], (DEPTH_2, DA_DH), 0.1),
        "da_subln_g": 1.0 + nrm(ks[14], (DEPTH_2, DA_VD), 0.05),
        "gm_ln_g": 1.0 + nrm(ks[15], (DEPTH_2, BRANCH_W), 0.05),
        "gm_ln_b": nrm(ks[16], (DEPTH_2, BRANCH_W), 0.02),
        "gm_w_s": nrm(ks[17], (DEPTH_2, GM_GROUPS, GM_CHUNK, GM_CHUNK), GM_CHUNK ** -0.5),
        "gm_b_s": 1.0 + nrm(ks[18], (DEPTH_2, GM_GROUPS, GM_CHUNK), 0.1),
        "w_branch": nrm(ks[19], (DEPTH_2, N_BRANCH, BRANCH_W, D), BRANCH_W ** -0.5),
        "w_out": nrm(ks[20], (DEPTH_2, D, D), D ** -0.5),
        "w_router": nrm(ks[21], (DEPTH_2, D, N_EXPERTS), D ** -0.5),
        "w_e1": nrm(ks[22], (DEPTH_2, N_EXPERTS, D, EXPERT_FF), D ** -0.5),
        "w_e3": nrm(ks[23], (DEPTH_2, N_EXPERTS, D, EXPERT_FF), D ** -0.5),
        "w_e2": nrm(ks[24], (DEPTH_2, N_EXPERTS, EXPERT_FF, D), EXPERT_FF ** -0.5),
        "g_final": 1.0 + nrm(ks[25], (D,), 0.05),
    }

def second_block(x, c, ctx, c_ctx, w_ada, b_ada, g_norm1, g_norm2, w_in, na_rpb,
              da_lam_q1, da_lam_k1, da_lam_q2, da_lam_k2, da_subln_g,
              gm_ln_g, gm_ln_b, gm_w_s, gm_b_s, w_branch, w_out,
              w_router, w_e1, w_e3, w_e2, g_final):
    L = x.shape[1]
    tabs = rope_tables(L)
    xc = ctx
    for i in range(DEPTH_2):
        last = i == DEPTH_2 - 1
        mod = jax.nn.silu(c) @ w_ada[i] + b_ada[i]
        sh1, sc1, gt1, sh2, sc2, gt2 = jnp.split(mod[:, None, :], N_MOD, axis=-1)
        modc = jax.nn.silu(c_ctx) @ w_ada[i] + b_ada[i]
        sh1c, sc1c, gt1c, sh2c, sc2c, gt2c = jnp.split(modc, N_MOD, axis=-1)
        lam_init = 0.8 - 0.6 * math.exp(-0.3 * i)
        lam = (jnp.exp(jnp.sum(da_lam_q1[i].astype(jnp.float32) * da_lam_k1[i].astype(jnp.float32)))
               - jnp.exp(jnp.sum(da_lam_q2[i].astype(jnp.float32) * da_lam_k2[i].astype(jnp.float32)))
               + lam_init)

        h = modulate(rmsnorm(x, g_norm1[i]), sh1, sc1)
        hc = modulate(rmsnorm(xc, g_norm1[i]), sh1c, sc1c)
        ka, va, kb, vb, qa, qb, u, v, gates = _split(h @ w_in[i], KV_SIZES + Q_SIZES)
        if last:
            kac, vac, kbc, vbc = _split(hc @ w_in[i][:, :KV_COLS], KV_SIZES)
        else:
            kac, vac, kbc, vbc, qac, qbc, uc, vcc, gatesc = _split(hc @ w_in[i], KV_SIZES + Q_SIZES)

        ya = neighbourhood_attn(_na_heads(qa), _na_heads(ka), _na_heads(va),
                                _na_heads(kac), _na_heads(vac), na_rpb[i])
        kb_all = jnp.concatenate([_da_qk(kbc), rope_2d(_da_qk(kb), tabs)], axis=1)
        vb_all = jnp.concatenate([_da_v(vbc), _da_v(vb)], axis=1)
        yb = diff_head_norm(diff_attn_blocks(rope_2d(_da_qk(qb), tabs), kb_all, vb_all, lam),
                            da_subln_g[i], lam_init)
        yc = gmlp_gate(jax.nn.gelu(u), jax.nn.gelu(v), gm_ln_g[i], gm_ln_b[i], gm_w_s[i], gm_b_s[i])
        x = x + gt1 * branch_merge(ya, yb, yc, gates, w_branch[i], w_out[i])
        if not last:
            yac = dense_attn(_na_heads(qac), _na_heads(kac), _na_heads(vac))
            ybc = diff_head_norm(diff_attend(_da_qk(qbc), _da_qk(kbc), _da_v(vbc), lam),
                                 da_subln_g[i], lam_init)
            ycc = gmlp_gate(jax.nn.gelu(uc), jax.nn.gelu(vcc), gm_ln_g[i], gm_ln_b[i], gm_w_s[i], gm_b_s[i])
            xc = xc + gt1c * branch_merge(yac, ybc, ycc, gatesc, w_branch[i], w_out[i])

        h2 = modulate(rmsnorm(x, g_norm2[i]), sh2, sc2)
        x = x + gt2 * ec_moe(h2, w_router[i], w_e1[i], w_e3[i], w_e2[i])
        if not last:
            h2c = modulate(rmsnorm(xc, g_norm2[i]), sh2c, sc2c)
            xc = xc + gt2c * ec_moe(h2c, w_router[i], w_e1[i], w_e3[i], w_e2[i])
    return rmsnorm(x, g_final)


def setup_inputs(seed=0):
    out = dict(first_inputs(seed))
    for name, value in second_inputs(seed + 1).items():
        if name != "x":
            out[name + "_2"] = value
    return out


def reference(
    x, meta_tokens, ln_in_g, ln_in_b, w_in, b_gate, conv_dw, conv_dw_b, conv_ln_g, conv_ln_b,
    w_conv_out, rwkv_mu, w0, w_decay_up, a0, a_up, g_up, k_k, k_a, r_k, lnx_g, lnx_b,
    w_rwkv_out, w_o, ln1_g, ln1_b, ffn_up, ffn_dw, ffn_down, ln2_g, ln2_b, c_2, ctx_2, c_ctx_2,
    w_ada_2, b_ada_2, g_norm1_2, g_norm2_2, w_in_2, na_rpb_2, da_lam_q1_2, da_lam_k1_2,
    da_lam_q2_2, da_lam_k2_2, da_subln_g_2, gm_ln_g_2, gm_ln_b_2, gm_w_s_2, gm_b_s_2,
    w_branch_2, w_out_2, w_router_2, w_e1_2, w_e3_2, w_e2_2, g_final_2,
):
    x = first_block(
        x, meta_tokens, ln_in_g, ln_in_b, w_in, b_gate, conv_dw, conv_dw_b, conv_ln_g,
        conv_ln_b, w_conv_out, rwkv_mu, w0, w_decay_up, a0, a_up, g_up, k_k, k_a, r_k, lnx_g,
        lnx_b, w_rwkv_out, w_o, ln1_g, ln1_b, ffn_up, ffn_dw, ffn_down, ln2_g, ln2_b,
    )
    return second_block(
        x, c_2, ctx_2, c_ctx_2, w_ada_2, b_ada_2, g_norm1_2, g_norm2_2, w_in_2, na_rpb_2,
        da_lam_q1_2, da_lam_k1_2, da_lam_q2_2, da_lam_k2_2, da_subln_g_2, gm_ln_g_2, gm_ln_b_2,
        gm_w_s_2, gm_b_s_2, w_branch_2, w_out_2, w_router_2, w_e1_2, w_e3_2, w_e2_2, g_final_2,
    )


_drawn_inputs = setup_inputs


def setup_inputs(seed=0):
    import zlib

    import numpy as np

    out = dict(_drawn_inputs(seed))
    spreads = {}
    factors = {'ctx_2': 4.238,
     'b_ada_2': 6.24,
     'g_norm1_2': 8.0,
     'g_norm2_2': 8.0,
     'na_rpb_2': 8.0,
     'da_lam_q1_2': 8.0,
     'da_lam_k1_2': 8.0,
     'da_lam_q2_2': 8.0,
     'da_lam_k2_2': 39.652,
     'da_subln_g_2': 8.0,
     'gm_ln_g_2': 8.0,
     'gm_ln_b_2': 8.0,
     'gm_b_s_2': 8.0}
    for name, (base, spread) in spreads.items():
        noise = np.random.default_rng([zlib.crc32(name.encode()), seed]).standard_normal(out[name].shape)
        drawn = base * np.exp(spread * noise) if base else spread * noise
        out[name] = jnp.asarray(drawn.astype(out[name].dtype))
    for name, factor in factors.items():
        out[name] = (out[name] * factor).astype(out[name].dtype)
    return out
```

```python
from contextlib import ExitStack

import numpy as np
import concourse.bass as bass
from concourse import mybir

F32 = mybir.dt.float32
U32 = mybir.dt.uint32
ALU = mybir.AluOpType
ACT = mybir.ActivationFunctionType
AX = mybir.AxisListType
ds = bass.ds

P = 128
D = 1024
KT = D // P
N_META = 16
SEQ = 512
T1 = N_META + SEQ
C1 = T1 // 2
CONV_K = 31
HEADS = 16
HD = 64
D_FF = 2816
FT = D_FF // P
FFN_K = 3
CH = 64
PADT = CH - N_META
TP = T1 + PADT
NCH = TP // CH
LEVELS = 6
ALPHA = 2.0 ** 0.25
LN_EPS, GN_EPS, RMS_EPS = 1e-5, 64e-5, 1e-6
EXP_HALF = float(np.exp(-0.5))
SLOT = 4096
BANK = 512


class Step:

    def __init__(self, eng, sem):
        self.eng, self.sem, self.n = eng, sem, 0

    def __call__(self, ins):
        ins.then_inc(self.sem, 1)
        self.n += 1
        return self.n

    def done(self, n=None):
        self.eng.wait_ge(self.sem, self.n if n is None else n)


def constants_one():
    i = np.arange(P)
    same = i[:, None] // HD == i[None, :] // HD
    s, t = i[:, None] % CH, i[None, :] % CH
    mask = np.where(i[None, :] < CH, s <= t, s < t)
    parts = [np.eye(P), np.full((P, P), 1.0 / D), same * 1.0, same / HD, mask * 1.0]
    for level in range(LEVELS):
        b = 1 << level
        parts.append((same & (s // (2 * b) == t // (2 * b)) & (s // b % 2 == 0) & (t // b % 2 == 1)) * 1.0)
    scan = np.ones((P, T1))
    scan[:, 0] = 0
    scan[:, N_META::CH] = 0
    parts.append(scan)
    return np.ascontiguousarray(np.concatenate(parts, 1).astype(np.float32))


DEPTH2 = 2
CTX = 256
T2 = CTX + SEQ
GRID_W, WIN_R, WIN_C = 64, 8, 16
BW = 512
NA_H, DA_H = 8, 4
N_EXP, EXP_FF = 16, 1024
CAP, CAPC = 2 * SEQ // N_EXP, 2 * CTX // N_EXP
NEG = -1e30
SQ_MAX = float(np.nextafter(np.float32(2.0 ** 64), np.float32(0)))
ROOT_SCALE = 2.0 ** -6
MEAN_MAX = 2.0 ** 121 * (1 - 2.0 ** -22)


def constants_two():
    i = np.arange(P)
    rot = np.zeros((P, P))
    first = i[i % 32 < 16]
    rot[first + 16, first] = -1
    rot[first, first + 16] = 1
    band = np.zeros((P, P))
    band[np.arange(2 * WIN_C - 1), 78 - np.arange(2 * WIN_C - 1)] = 1
    c, k = i[:, None] % GRID_W, np.arange(GRID_W)[None, :]
    start = np.clip(c - WIN_C // 2, 0, GRID_W - WIN_C)
    window = np.where((k >= start) & (k < start + WIN_C), 0.0, NEG)
    count = i[:, None] + P * np.arange(SEQ // P)[None, :]
    tokens = np.broadcast_to(np.arange(SEQ)[None, :], (P, SEQ))
    f = np.float32
    inv = f(10000.0) ** (-np.arange(0, 32, 2, dtype=f) / f(32))
    t = np.arange(SEQ)
    pos = np.where((i[:, None] % 64) < 32, t // GRID_W, t % GRID_W).astype(f)
    angle = pos * inv[i % 16][:, None]
    parts = [rot, np.full((P, P), 1.0 / P), band, window, count, tokens, np.cos(angle), np.sin(angle)]
    return np.ascontiguousarray(np.concatenate([p.astype(f) for p in parts], 1))


class Dense:

    def __init__(self, slabs, tps, kt, chunks, dmas=1, cols=None):
        self.slabs, self.tps, self.kt, self.chunks, self.dmas = slabs, tps, kt, chunks, dmas
        self.cols = cols or tps * P


def plan(stages):
    tile, slot, used, last = 0, 0, [0, 0], [0, 0]
    for s in stages.values():
        s.tile0, s.slot0, s.used0, s.last0 = tile, slot, list(used), list(last)
        for n in range(s.slabs):
            used[slot] += s.dmas
            last[slot] = tile + s.tps
            tile += s.tps
            slot ^= 1
        s.tile1 = tile


def build(nc, I, out):
    ctx = ExitStack()
    sems = {}

    def S(name):
        if name not in sems:
            sems[name] = nc.alloc_semaphore(name)
        return sems[name]

    A = ctx.enter_context(nc.sbuf_tensor("arena", [P, 53200], F32))
    PS = ctx.enter_context(nc.psum_tensor("psum", [P, 8, BANK], F32))

    def sb(off, n, p0=0, p1=P):
        return A[p0:p1, off:off + n]

    PAR = 0
    IDN, OND, BON, BOM, MSK, LVL = 1024, 1152, 1280, 1408, 1536, 1664
    SCM = LVL + LEVELS * P
    N_CONST = SCM + T1 - IDN
    RING = 2960
    H = RING + 2 * SLOT
    CS = H + KT * T1
    R_, K_, V_ = CS + KT * T1, CS + KT * T1 + KT * TP, CS + KT * T1 + 2 * KT * TP
    A_, B_ = V_ + KT * TP, V_ + 2 * KT * TP
    LO = B_ + KT * TP
    PL = LO + 1600
    BNS = LO + 1680
    TMP = BNS + KT * T1
    assert TMP + 4608 <= 53200
    ident, ones_d, ones_h, mean_h = (sb(o, P) for o in (IDN, OND, BON, BOM))
    slot = [sb(RING + s * SLOT, SLOT) for s in range(2)]

    rows, col, dram_rows = 0, {}, []

    def param(name, ap, n):
        nonlocal rows
        col[name] = PAR + rows
        dram_rows.append((rows, ap, n))
        rows += n

    def vec(ap):
        return ap.rearrange("(n p) -> n p", p=P)

    param("ln_in_g", vec(I["ln_in_g"]), KT)
    param("ln_in_b", vec(I["ln_in_b"]), KT)
    param("conv_w", I["conv_dw"][0].rearrange("j (i p) -> (j i) p", p=P), CONV_K * KT)
    mu_full = 3 * KT + 2
    for n in ("conv_dw_b", "conv_ln_g", "conv_ln_b", "w0", "a0", "k_k", "k_a", "lnx_g", "lnx_b", "ln1_g", "ln1_b",
              "ln2_g", "ln2_b"):
        param(n, vec(I[n][0]), KT)
    param("b_gate", vec(I["b_gate"][0]), 2 * KT)
    param("r_k", I["r_k"][0].rearrange("(i h) n -> i (h n)", h=2), KT)
    param("ffn_dw", I["ffn_dw"][0].rearrange("j (i p) -> (j i) p", p=P), FFN_K * 2 * FT)
    param("mu", vec(I["rwkv_mu"][0][0:mu_full * P]), mu_full)
    param("mu_last", I["rwkv_mu"][0:1, mu_full * P:], 1)
    for l in range(DEPTH2):
        param(f"g_norm1{l}", vec(I["g_norm1_2"][l]), KT)
        param(f"g_norm2{l}", vec(I["g_norm2_2"][l]), KT)
        param(f"b_ada{l}", vec(I["b_ada_2"][l]), 6 * KT)
        param(f"subln{l}", I["da_subln_g_2"][l:l + 1, :], 1)
    param("g_final", vec(I["g_final_2"]), KT)
    param("c", vec(I["c_2"][0]), KT)
    param("c_ctx", vec(I["c_ctx_2"]), KT)
    n_par = -(-rows // P)
    assert rows <= 800

    def pc(name, i=0, p1=P):
        c = col[name] + i
        return A[0:p1, c:c + 1]

    X2 = CS
    HB = X2 + KT * T2
    YA, YB, YC = (HB + KT * T2 + n * 4 * T2 for n in range(3))
    QR, KR, VR = (HB + KT * T2 + (3 + n) * 4 * T2 for n in range(3))
    SCR = VR + 4 * T2
    TAIL = SCR + 6400
    MERGED, GATE, PROD = QR, QR + KT * T2, H
    ROT, O128, BAND, WIN, CNT, TOK = 1280, 1408, 1536, 1664, 1728, 1732
    N_CONST2 = TOK + SEQ - ROT
    AMT, ASC = TOK + SEQ, TOK + SEQ + 2 * P
    MOD, SG1, SG2 = PAR + 800, PAR + 896, PAR + 912
    LAMC, SUBC = PAR + 928, PAR + 930
    idx_dram = nc.dram_tensor("expert_tokens", (N_EXP, CAP + CAPC), F32, kind="Internal").ap()

    two = [(0, C1), (C1, C1)]
    st = {
        "glu_a": Dense(2, 4, KT, two), "glu_g": Dense(2, 4, KT, two), "rkv": Dense(6, 4, KT, two),
        "lora": Dense(1, 3, KT, two), "lora_up": Dense(1, 0, 1, two, dmas=2),
        "g_up": Dense(1, 8, 2, two, dmas=2), "gates": Dense(4, 4, KT, two),
        "conv_out": Dense(2, 4, KT, two), "rwkv_out": Dense(2, 4, KT, two), "w_o": Dense(2, 4, KT, two),
        "ffn_up": Dense(11, 4, KT, two, dmas=2), "ffn_down": Dense(8, 1, FT, two),
    }
    everything, xs_only = [(0, T2 // 2), (T2 // 2, T2 // 2)], [(CTX, SEQ)]
    for l in range(DEPTH2):
        q = everything if l < DEPTH2 - 1 else xs_only
        nt = T2 // P if l < DEPTH2 - 1 else SEQ // P
        st[f"ada{l}"] = Dense(12, 1, KT, [(0, P)], cols=BW)
        st[f"u{l}"] = Dense(1, 4, KT, q)
        st[f"v{l}"] = Dense(1, nt, KT, [(0, BW)], cols=BW)
        st[f"ka{l}"] = Dense(1, 4, KT, everything)
        st[f"va{l}"] = Dense(1, T2 // P, KT, [(0, BW)], cols=BW)
        st[f"qa{l}"] = Dense(1, 4, KT, q)
        st[f"kb{l}"] = Dense(1, 4, KT, everything)
        st[f"vb{l}"] = Dense(1, T2 // P, KT, [(0, BW)], cols=BW)
        st[f"qb{l}"] = Dense(1, 4, KT, q)
        for b in range(3):
            st[f"gate{b}{l}"] = Dense(2, 4, KT, q)
            st[f"branch{b}{l}"] = Dense(1, 8, BW // P, q)
        st[f"out{l}"] = Dense(2, 4, KT, q)
    plan(st)
    FULL0, FREE0 = 16, 2

    def w_slab(s):
        return lambda q: slot[q][:, 0:s.kt * s.cols].rearrange("p (k n) -> p k n", k=s.kt)

    def columns(w, n0, n):
        return w[:, n0 * P:n0 * P + n] if isinstance(n0, int) else w[:, ds(n0 * P, n)]

    def stream(sp, name, src, pre=()):
        s = st[name]
        for sem, v in pre:
            sp.wait_ge(sem, v)

        def one(n, u):
            q = (s.slot0 + u) % 2
            if isinstance(n, int) and n < 2:
                if s.last0[q]:
                    sp.wait_ge(S("acc_full"), FULL0 + s.last0[q])
            else:
                sp.wait_ge(S("acc_full"), (n - 1) * s.tps + (FULL0 + s.tile0))
            for dst, ap in src(n, slot[q]):
                sp.dma_start(dst, ap).then_inc(S(f"w_in{q}"), 16)

        loop(sp, s.slabs, one)

    def loop(eng, n, one, straight=False):
        head = n if straight else min(n, 2)
        for u in range(head):
            one(u, u % 2)
        pairs = (n - head) // 2
        if pairs:
            with eng.Fori(1, 1 + pairs) as it:
                for u in range(2):
                    one(it * 2 + u, u)
        if (n - head) % 2:
            one(n - 1, (n - 1) % 2)

    def products(pe, name, rhs, pre=(), width=None, depth=None, beside=None, first=None):
        s = st[name]
        for sem, v in pre:
            pe.wait_ge(sem, v)

        def one(n, u):
            q = (s.slot0 + u) % 2
            w = w_slab(s)(q)
            pe.wait_ge(S(f"w_in{q}"), (n - u) * (8 * s.dmas) + 16 * (s.used0[q] + s.dmas))
            for j in range(s.tps):
                region = (s.tile0 + u * s.tps + j) % 2
                m = width[j] if width else P
                pe.wait_ge(S("acc_free"), n * s.tps + (s.tile0 + j + 1 + (FREE0 - 2)))
                for c, (c0, cn) in enumerate(s.chunks):
                    for k in range(s.kt):
                        kp = depth[k] if depth else P
                        if first and isinstance(n, int) and n == 0 and j == 0 and c == 0:
                            pe.wait_ge(*first(k))
                        mm = pe.matmul(PS[0:m, 2 * region + c, 0:cn], w[0:kp, k, j * P:j * P + m], rhs(k, c0, cn),
                                       start=(k == 0), stop=(k == s.kt - 1))
                mm.then_inc(S("acc_full"), 1)
                if beside:
                    beside(n * s.tps + j)

        loop(pe, s.slabs, one, straight=beside is not None)

    def take(act, name, evac, pre=(), width=None, free=None, after=None, beside=None):
        s = st[name]
        for sem, v in pre:
            act.wait_ge(sem, v)

        def one(n, u):
            if free:
                free(n)
            for j in range(s.tps):
                region = (s.tile0 + u * s.tps + j) % 2
                m = width[j] if width else P
                act.wait_ge(S("acc_full"), n * s.tps + (s.tile0 + j + 1 + FULL0))
                acc = PS[0:m, 2 * region:2 * region + len(s.chunks), 0:s.chunks[0][1]]
                evac(n * s.tps + j, acc, u * s.tps + j).then_inc(S("acc_free"), 1)
                if beside:
                    beside(n * s.tps + j)
            if after:
                after(n, u)

        loop(act, s.slabs, one, straight=beside is not None)

    def taken(name, n=None):
        s = st[name]
        return S("acc_free"), FREE0 + s.tile0 + (s.tile1 - s.tile0 if n is None else n)

    def at(off, n, p0=0, p1=P):
        return A[p0:p1, off:off + n] if isinstance(off, int) else A[p0:p1, ds(off, n)]

    def halves(ap):
        return ap.rearrange("p (c n) -> p c n", c=2)

    ln_n = {"pe": 0, "act": 0, "dve": 0}
    SQ, RSTD = TMP, TMP + 1536
    LNB = [SQ, RSTD]

    def stat(b, t):
        return PS[:, b:b + 2, 0:t // 2]

    def ln_pe(pe, x, t, pre, center=True):
        n = ln_n["pe"]
        ln_n["pe"] += 1
        for sem, v in pre:
            pe.wait_ge(sem, v)
        c = t // 2
        if center:
            for h in range(2):
                for k in range(KT):
                    mm = pe.matmul(PS[:, 4 + h, 0:c], ones_d, at(x(k) + h * c, c), start=(k == 0), stop=(k == KT - 1))
            mm.then_inc(S("ln_sum"), 1)
        else:
            pe.nop().then_inc(S("ln_sum"), 1)
        for k in range(KT):
            pe.wait_ge(S("ln_sq"), n * KT + k + 1)
            for h in range(2):
                mm = pe.matmul(PS[:, 6 + h, 0:c], ones_d, at(LNB[0] + k % 2 * t + h * c, c), start=(k == 0), stop=(k == KT - 1))
            mm.then_inc(S("ln_sq_used"), 1)

    def ln_dve(dve, step, x, xn, t, eps, center=True, pre=()):
        n = ln_n["dve"]
        ln_n["dve"] += 1
        for sem, v in pre:
            dve.wait_ge(sem, v)
        if center:
            dve.wait_ge(S("ln_sum"), n + 1)
            for k in range(KT):
                nc.vector.tensor_tensor(halves(at(xn(k), t)), halves(at(x(k), t)), stat(4, t), ALU.subtract)\
                    .then_inc(S("ln_cent"), 1)
        else:
            dve.nop().then_inc(S("ln_cent"), KT)
        dve.wait_ge(S("ln_sq_used"), (n + 1) * KT)
        rstd = at(LNB[1], t)
        nc.vector.tensor_scalar(halves(rstd), stat(6, t), eps, None, ALU.add).then_inc(S("ln_var"), 1)
        dve.wait_ge(S("ln_sd"), n + 1)
        step(nc.vector.reciprocal(rstd, rstd))
        step.done()
        dve.wait_ge(S("ln_cent"), (n + 1) * KT)
        for k in range(KT):
            src = xn(k) if center else x(k)
            nc.vector.tensor_tensor(at(xn(k), t), at(src, t), rstd, ALU.mult).then_inc(S("ln_norm"), 1)

    def ln_act(act, x, xn, t, put, per=1, center=True, pre=()):
        n = ln_n["act"]
        ln_n["act"] += 1
        for sem, v in pre:
            act.wait_ge(sem, v)
        for k in range(KT):
            if center:
                act.wait_ge(S("ln_cent"), n * KT + k + 1)
            if n * KT + k >= 2:
                act.wait_ge(S("ln_sq_used"), n * KT + k - 1)
            src = xn(k) if center else x(k)
            nc.scalar.activation(at(LNB[0] + k % 2 * t, t), at(src, t), ACT.Square).then_inc(S("ln_sq"), 1)
        act.wait_ge(S("ln_var"), n + 1)
        nc.scalar.activation(at(LNB[1], t), at(LNB[1], t), ACT.Sqrt).then_inc(S("ln_sd"), 1)
        for k in range(KT):
            act.wait_ge(S("ln_norm"), n * KT + k + 1)
            put(k).then_inc(S("ln_out"), 1)

    def ln_tile(n):
        return lambda k: (S("ln_out"), n * KT + k + 1)

    def ln_done(n):
        return S("ln_out"), (n + 1) * KT

    total, base = {}, {}
    LNB2 = [SCR + 4096, SCR + 4096 + 2 * T2]
    dve_steps = [0]

    def inc(ins, name, n=1, times=1):
        total[name] = total.get(name, 0) + n * times
        return ins.then_inc(S(name), n)

    def wt(eng, name, v):
        eng.wait_ge(S(name), v + base.get(name, 0))

    def spread(ap, n):
        return ap.rearrange("p (c n) -> p c n", c=n)

    def attention_units(l):
        last = l == DEPTH2 - 1
        q_ctx = [] if last else [0, P]
        na, da = [], []
        for h in range(NA_H):
            p0, i = h % 2 * HD, h // 2
            row = lambda o, c, n: A[p0:p0 + HD, o + i * T2 + c:o + i * T2 + c + n]
            for q in q_ctx + [CTX + n * P for n in range(SEQ // P)]:
                own = q < CTX
                j0 = WIN_R - 1 - 2 * ((q - CTX) // P)
                bias = None if own else (h, j0)
                na.append(dict(maps=[(row(QR, q, P), row(KR, 0, CTX), None if own else row(KR, CTX, SEQ))], bias=bias,
                               nk=2 if own else 6, v=lambda t, h=h: at(VR + t * BW + h * HD, HD), m=HD, p0=p0,
                               out=row(YA, q, P)))
        for h in range(DA_H):
            for q in q_ctx + [CTX + n * P for n in range(SEQ // P)]:
                own = q < CTX
                maps = []
                for p0 in (0, HD):
                    row = lambda o, c, n: A[p0:p0 + HD, o + h * T2 + c:o + h * T2 + c + n]
                    maps.append((row(QR, q, P), row(KR, 0, CTX), None if own else row(KR, CTX, SEQ)))
                da.append(dict(maps=maps, bias=None, nk=2 if own else 6, v=lambda t, h=h: at(VR + t * BW + h * P, P), m=P,
                               p0=0, out=at(YB + h * T2 + q, P)))
        return na, da

    def counts(units):
        jobs = [(n, kx is not None) for n, u in enumerate(units) for _, _, kx in u["maps"]]
        seq_jobs = [sum(s for _, s in jobs[j % 2:j + 1:2]) for j in range(len(jobs))]
        seq_units = [sum(u["nk"] > 4 for u in units[:n + 1]) for n in range(len(units))]
        return seq_jobs, seq_units

    def layer(l):
        last = l == DEPTH2 - 1
        base.clear()
        base.update(total)
        LNB[:] = LNB2
        q0 = CTX if last else 0
        nq = T2 - q0
        nqc = 1 if last else 2
        tok = list(range(q0 // P, T2 // P))
        na, da = attention_units(l)
        xk = lambda k: X2 + k * T2
        hb = lambda k: HB + k * T2
        xq = lambda k: X2 + k * T2 + q0
        hq = lambda k: HB + k * T2 + q0
        mod = lambda m, k, v: at(MOD + (m * KT + k) * 2 + v, 1)
        mod8 = lambda m: at(MOD + m * KT * 2, KT * 2).rearrange("p (k v) -> p k v", v=2)
        s_ada = st[f"ada{l}"]
        mt = [at(AMT + u * P, P) for u in range(2)]
        GMG, GMB, BSR, WS, WST = SCR, SCR + BW, SCR + 2 * BW, SCR + 3 * BW, SCR + 4 * BW
        RPB, RPT, LAM, LAMS, WR = TAIL, TAIL + 32, TAIL + 160, TAIL + 416, TAIL + 432
        GST = LAMS + 4
        assert TAIL + 584 <= 53200
        CELLS = TAIL + 560
        NA_S = lambda j: SCR + 4096 + j % 3 * T2
        DA_S = lambda j: SCR + j % 6 * T2
        NA_P = lambda n: YB + n % 2 * T2
        DA_P = lambda n: SCR + 6 * T2 + n % 2 * T2
        COS, SIN = H, H + SEQ
        SUB = SCR + KT * T2 // 2
        half_bm = NA_H // 2
        bm = [A[:, o:o + half_bm * 1024].rearrange("p (h j c) -> p h j c", h=half_bm, c=GRID_W) for o in (H, SCR)]
        DA_SCALE = NA_SCALE = HD ** -0.5
        n_norm = [ln_n["pe"]]
        HT, PG, PGC, IB = HB + KT * T2, HB + 2 * KT * T2, HB + 2 * KT * T2 + 4096, HB + 2 * KT * T2 + 5120
        XIN, XINC = IB + 1536, IB + 1536 + 8192
        ES = [RING, RING + SLOT] + [HB + n * SLOT for n in range(4)]
        HID = [PGC, H]
        AFF, AFT, WRK, VAL, IDX = H, H + 96, H + 96 + T2, H + 96 + 2 * T2, H + 192 + 2 * T2
        IDF, GTF, COL = H + 288 + 2 * T2, H + 544 + 2 * T2, H + 4160
        ROWS, YCG = COL - 16, HB + SLOT
        kinds = [("x", CTX, SEQ, CAP, 2)] + ([] if last else [("c", 0, CTX, CAPC, 4)])
        PTG = HB
        block = nc.Block()
        block.__enter__()

        @block.sync
        def _(sp):
            n_small = 0

            def small(dst, src):
                nonlocal n_small
                n_small += 1
                inc(sp.dma_start(dst, src), "small_in", 16)

            if l == 0:
                inc(sp.dma_start(A[:, ROT:ROT + N_CONST2], I["const2"][:, 0:N_CONST2]), "const2_in", 16)
                inc(sp.dma_start(at(YA, 2 * D).rearrange("p (t c) -> p t c", t=2),
                                 I["ctx_2"][0].rearrange("(t p) c -> p t c", p=P)), "ctx_in", 16)
            cols = lambda w, first: (lambda n, dst: [(
                dst.rearrange("p (k n) -> p k n", k=KT),
                (w[:, :, n * BW + first:n * BW + first + BW] if isinstance(n, int) else w[:, :, ds(n * BW + first, BW)]))])
            view = lambda w: w.rearrange("(k p) n -> p k n", p=P)
            over = lambda row: row.partition_broadcast(P)
            stream(sp, f"ada{l}", cols(view(I["w_ada_2"][l]), 0))
            small(at(GMG, BW), over(I["gm_ln_g_2"][l]))
            small(at(GMB, BW), over(I["gm_ln_b_2"][l]))
            small(at(BSR, BW), over(I["gm_b_s_2"][l].rearrange("g p -> (g p)")))
            small(at(WS, BW).rearrange("p (g q) -> p g q", g=4), I["gm_w_s_2"][l].rearrange("g p q -> p g q"))
            small(A[0:120, RPB:RPB + 31], I["na_rpb_2"][l].rearrange("h r c -> (h r) c"))
            for n, x in enumerate(("q1", "k1", "q2", "k2")):
                small(at(LAM + n * HD, HD), over(I[f"da_lam_{x}_2"][l]))
            small(at(WR, KT * N_EXP).rearrange("p (k e) -> p k e", k=KT), view(I["w_router_2"][l]))
            w_in = view(I["w_in_2"][l])
            for n, c in (("u", 6), ("v", 7), ("ka", 0), ("va", 1), ("qa", 4), ("kb", 2), ("vb", 3), ("qb", 5)):
                stream(sp, f"{n}{l}", cols(w_in, c * BW))
            for b in range(3):
                stream(sp, f"gate{b}{l}", cols(w_in, 8 * BW + b * D))
                stream(sp, f"branch{b}{l}", lambda n, dst: [(
                    dst.rearrange("p (k n) -> p k n", k=BW // P), view(I["w_branch_2"][l, b]))])
            stream(sp, f"out{l}", cols(view(I["w_out_2"][l]), 0))

            def slab(e, m, half):
                w = I[("w_e1_2", "w_e3_2", "w_e2_2")[m]][l].rearrange("e (k p) n -> p (e k) n", p=P)
                k0 = e * KT + half * 4
                src = w[:, k0:k0 + 4, :] if isinstance(k0, int) else w[:, ds(k0, 4), :]
                n = 2 * m + half
                return sp.dma_start(at(ES[n], SLOT).rearrange("p (k n) -> p k n", k=4), src), f"expert_in{n}"

            sp.wait_ge(S("acc_full"), FULL0 + st[f"out{l}"].tile1)
            for n in range(2):
                inc(*slab(0, 0, n), 16, N_EXP)
            wt(sp, "chosen", 1)
            for n, (_, _, _, cap, _) in enumerate(kinds):
                inc(sp.dma_start(idx_dram[:, n * CAP:n * CAP + cap], A[0:N_EXP, IDF + n * P:IDF + n * P + cap]), "idx_out", 16)
            wt(sp, "idx_out", 16 * len(kinds))
            for n, (_, _, _, cap, _) in enumerate(kinds):
                inc(sp.dma_start(at(IB + n * N_EXP * CAP, N_EXP * cap).rearrange("p (e s) -> p e s", e=N_EXP),
                                 idx_dram[:, n * CAP:n * CAP + cap].partition_broadcast(P)), "idx_in", 16)
            wt(sp, "gathered", 1)
            for n in range(2, 6):
                inc(*slab(0, n // 2, n % 2), 16, N_EXP)
            with sp.Fori(1, N_EXP) as e:
                for n in range(6):
                    if n < 5:
                        wt(sp, "expert_used", e * 5 + (n - 4))
                    else:
                        wt(sp, "ye_made", e + 2)
                    ins, name = slab(e, n // 2, n % 2)
                    ins.then_inc(S(name), 16)
            if last:
                for t in range(SEQ // P):
                    wt(sp, "final", 2 * t + 2)
                    inc(sp.dma_start(out[0, t * P:t * P + P, :], at(HT + t * D, D)), "out_done", 16)
                wt(sp, "out_done", 16 * SEQ // P)

        n_small = 10
        @block.tensor
        def _(pe):
            if l == 0:
                wt(pe, "ctx_in", 16)
                for k in range(KT):
                    if k >= 2:
                        wt(pe, "ctx_taken", k - 1)
                    for t in range(2):
                        tr = pe.transpose(PS[:, 4 + k % 2, t * P:t * P + P], at(YA + t * D + k * P, P), ident)
                    inc(tr, "ctx_turned")
            wt(pe, "ada_c", 2)

            def ada_turn(n, u):
                pe.wait_ge(S("acc_free"), n + (FREE0 + s_ada.tile0 + 1))
                if not isinstance(n, int) or n >= 2:
                    wt(pe, "ada_mod", n - 1)
                pe.transpose(PS[:, 4 + u, 0:P], mt[u], ident).then_inc(S("ada_turned"), 1)

            def ada_one(n, u):
                q = (s_ada.slot0 + u) % 2
                r = (s_ada.tile0 + u) % 2
                w = slot[q].rearrange("p (k n) -> p k n", k=KT)
                pe.wait_ge(S(f"w_in{q}"), (n - u) * 8 + 16 * (s_ada.used0[q] + 1))
                pe.wait_ge(S("acc_free"), n + (s_ada.tile0 + 1 + FREE0 - 2))
                for k in range(KT):
                    for g in range(4):
                        mm = pe.matmul(PS[g * 32:g * 32 + 32, 2 * r, 0:P], at(ASC + k * 32, 32), w[:, k, g * P:g * P + P],
                                       start=(k == 0), stop=(k == KT - 1))
                mm.then_inc(S("acc_full"), 1)
                if not isinstance(n, int) or n >= 1:
                    ada_turn(n - 1, 1 - u)
            loop(pe, s_ada.slabs, ada_one)
            ada_turn(s_ada.slabs - 1, (s_ada.slabs - 1) % 2)
            total["ada_turned"] = total.get("ada_turned", 0) + s_ada.slabs

            rhs = lambda k, c0, cn: at(hb(k) + c0, cn)

            def by_token(name, tiles):
                s = st[name]
                q = s.slot0
                w = slot[q].rearrange("p (k n) -> p k n", k=KT)
                pe.wait_ge(S(f"w_in{q}"), 16 * (s.used0[q] + 1))
                for n, t in enumerate(tiles):
                    r = (s.tile0 + n) % 2
                    pe.wait_ge(S("acc_free"), s.tile0 + n + 1 + FREE0 - 2)
                    for k in range(KT):
                        mm = pe.matmul(PS[:, 2 * r, :], at(hb(k) + t * P, P), w[:, k, :], start=(k == 0), stop=(k == KT - 1))
                    mm.then_inc(S("acc_full"), 1)

            ln_pe(pe, xk, T2, [(S("mod_ready"), base.get("mod_ready", 0) + 1)], center=False)
            products(pe, f"u{l}", rhs, first=ln_tile(n_norm[0]))
            by_token(f"v{l}", tok)
            wt(pe, "small_in", 16 * n_small)
            for g in range(4):
                tr = pe.transpose(PS[:, 4, g * P:g * P + P], at(WS + g * P, P), ident)
            inc(tr, "ws_turned")
            wt(pe, "ws_taken", 1)
            wt(pe, "gm_normed", len(tok))
            for g in range(4):
                if g >= 2:
                    wt(pe, "gm_done", g - 1)
                for n in range(len(tok)):
                    b = 4 + g % 2 * 2 + n // 4
                    mm = pe.matmul(PS[:, b, n % 4 * P:n % 4 * P + P], at(VR + n * BW + g * P, P), at(WST + g * P, P),
                                   start=True, stop=True)
                inc(mm, "gm_mixed")
            products(pe, f"ka{l}", rhs)
            by_token(f"va{l}", range(T2 // P))
            products(pe, f"qa{l}", rhs)
            wt(pe, "gm_done", 4)
            inc(pe.transpose(PS[0:31, 4, 0:120], A[0:120, RPB:RPB + 31], ident[0:120, 0:120]), "rpb_turned")
            wt(pe, "rpb_taken", 1)
            for c4 in range(GRID_W // 4):
                if c4 >= 4:
                    wt(pe, "bias_taken", 4 * (c4 - 3))
                for j in range(4):
                    c = c4 * 4 + j
                    for p0 in (0, HD):
                        mm = pe.matmul(PS[p0:p0 + HD, 4 + c4 % 4, j * 120:j * 120 + 120],
                                       A[0:31, BAND + 63 - c:BAND + 127 - c], A[0:31, RPT:RPT + 120], start=True, stop=True)
                inc(mm, "bias_made")

            def attend(units, a, s_at, p_at):
                j, n_u = 0, len(units)
                seq_jobs, seq_units = counts(units)
                for n in range(n_u + 3):
                    if n < n_u:
                        for q, kc, kx in units[n]["maps"]:
                            half = j % 2
                            if j >= 2:
                                wt(pe, f"{a}_ctx{half}", j // 2)
                                if seq_jobs[j - 2]:
                                    wt(pe, f"{a}_seq{half}", seq_jobs[j - 2])
                            inc(pe.matmul(PS[:, 2 * half, 0:CTX], q, kc, start=True, stop=True), f"{a}_sc{half}")
                            if kx is not None:
                                inc(pe.matmul(PS[:, 2 * half + 1, :], q, kx, start=True, stop=True), f"{a}_ss{half}")
                            j += 1
                    if n >= 3:
                        wt(pe, f"{a}_pt0", n - 2)
                        if seq_units[n - 3]:
                            wt(pe, f"{a}_pt1", seq_units[n - 3])
                    if 2 <= n <= n_u + 1:
                        u = units[n - 2]
                        src = s_at((n - 2) * len(u["maps"]))
                        wt(pe, f"{a}_p", n - 1)
                        for t in range(u["nk"]):
                            tr = pe.transpose(PS[:, 4 + t // 4, t % 4 * P:t % 4 * P + P], at(src + t * P, P), ident)
                            if t == min(3, u["nk"] - 1):
                                inc(tr, f"{a}_t0")
                        if u["nk"] > 4:
                            inc(tr, f"{a}_t1")
                    if n >= 3:
                        u = units[n - 3]
                        if n >= 5:
                            wt(pe, f"{a}_out", n - 4)
                        for t in range(u["nk"]):
                            mm = pe.matmul(PS[u["p0"]:u["p0"] + u["m"], 6 + n % 2, 0:P], u["v"](t),
                                           at(p_at(n - 3) + t * P, P), start=(t == 0), stop=(t == u["nk"] - 1))
                        inc(mm, f"{a}_o")

            pe.wait_ge(*taken(f"qa{l}"))
            wt(pe, "bias_taken", 4 * (GRID_W // 4))
            attend(na, "na", NA_S, NA_P)
            wt(pe, "na_out", len(na))
            products(pe, f"kb{l}", rhs)
            by_token(f"vb{l}", range(T2 // P))
            products(pe, f"qb{l}", rhs)
            pe.wait_ge(*taken(f"qb{l}"))
            for n in range(8):
                if n >= 4:
                    wt(pe, "rope_t", n - 3)
                r = (KR if n < 4 else QR) + n % 4 * T2 + CTX
                inc(pe.matmul(PS[:, 4 + n % 4, :], sb(ROT, P), at(r, SEQ), start=True, stop=True), "rope_r")
            wt(pe, "rope_done", 8)
            attend(da, "da", DA_S, DA_P)
            def sub_beside(t):
                h = t // 2
                if t % 2 == 0:
                    wt(pe, "sub_sq", h + 1)
                    if h >= 2:
                        wt(pe, "sub_rstd", h - 1)
                    for c in range(2):
                        mm = pe.matmul(PS[:, 4 + h % 2 * 2 + c, 0:nq // 2], sb(O128, P),
                                       at(SUB + h % 2 * T2 + c * (nq // 2), nq // 2), start=True, stop=True)
                    inc(mm, "sub_sum")
            for b, y in enumerate((YA, YB, YC)):
                products(pe, f"gate{b}{l}", rhs, beside=None if b else sub_beside)
                pre = [(S("sub_out"), base.get("sub_out", 0) + DA_H)] if b == 1 else []
                products(pe, f"branch{b}{l}", lambda k, c0, cn: at(y + k * T2 + c0, cn), pre)
            products(pe, f"out{l}", lambda k, c0, cn: at(MERGED + k * T2 + c0, cn),
                     first=lambda k: (S("merge"), base.get("merge", 0) + 2 * KT + k + 1))
            ln_pe(pe, xq, nq, [(S("attn_res"), base.get("attn_res", 0) + KT * (1 if last else 2))], center=False)
            pe.wait_ge(*ln_done(n_norm[0] + 1))
            for n, t in enumerate(tok):
                for k in range(KT):
                    mm = pe.matmul(PS[:, 4, n * N_EXP:(n + 1) * N_EXP], at(hb(k) + t * P, P), at(WR + k * N_EXP, N_EXP),
                                   start=(k == 0), stop=(k == KT - 1))
            inc(mm, "logits")
            for n, t in enumerate(tok):
                for half in range(2):
                    m = 2 * n + half
                    b = m % 4
                    if m >= 4:
                        wt(pe, "ht_taken", m - 3)
                    for k in range(4):
                        tr = pe.transpose(PS[:, b, k * P:k * P + P], at(hb(half * 4 + k) + t * P, P), ident)
                    inc(tr, "ht_turned")
            wt(pe, "aff", 1)
            for n, t in enumerate(tok):
                tr = pe.transpose(PS[0:N_EXP, 5 + n // 4, n % 4 * P:n % 4 * P + P], at(AFF + n * N_EXP, N_EXP), ident)
            inc(tr, "aff_turned")
            wt(pe, "chosen", 1)
            for n in range(len(kinds)):
                for m, o in enumerate((IDF, GTF)):
                    tr = pe.transpose(PS[:, 4, (2 * n + m) * N_EXP:(2 * n + m + 1) * N_EXP],
                                      A[0:N_EXP, o + n * P:o + n * P + P], ident[0:N_EXP, 0:N_EXP])
            inc(tr, "col_turned")
            wt(pe, "ht_taken", 2 * len(tok))
            wt(pe, "onehot", SEQ // P + (0 if last else CTX // P))
            x0 = len(tok) - SEQ // P
            m = 0
            for k in range(KT):
                for half in range(2):
                    if m >= 4:
                        wt(pe, "xin", m - 3)
                    for t in range(SEQ // P):
                        mm = pe.matmul(PS[:, m % 4, :], at(HT + (x0 + t) * D + k * P, P), at(PG + t * D + half * BW, BW),
                                       start=(t == 0), stop=(t == SEQ // P - 1))
                    inc(mm, "xin_made")
                    m += 1
                if not last:
                    if m >= 4:
                        wt(pe, "xin", m - 3)
                    for t in range(CTX // P):
                        mm = pe.matmul(PS[:, m % 4, :], at(HT + t * D + k * P, P), at(PGC + t * BW, BW),
                                       start=(t == 0), stop=(t == CTX // P - 1))
                    inc(mm, "xin_made")
                    m += 1
            wt(pe, "xin", m)
            inc(pe.nop(), "gathered")
            inc(pe.nop(), "ye_made", 2)
            with pe.Fori(0, N_EXP // 2) as e2:
                for u in range(2):
                    b = 4 * u
                    e = e2 * 2 + u
                    hid = HID[u]
                    xs = hid + 3 * BW
                    wt(pe, "xs", e + 1)
                    wt(pe, "ye", e + 1)
                    for m in range(2):
                        for half in range(2):
                            n = 2 * m + half
                            w = at(ES[n], SLOT).rearrange("p (k n) -> p k n", k=4)
                            pe.wait_ge(S(f"expert_in{n}"), e * 16 + (16 + base.get(f"expert_in{n}", 0)))
                            for k in range(4):
                                kk = half * 4 + k
                                for c in range(2):
                                    mm = pe.matmul(PS[c * HD:c * HD + HD, b + m, :], at(xs + kk * CAP, CAP),
                                                   w[:, k, c * BW:c * BW + BW], start=(kk == 0), stop=(kk == KT - 1))
                            if not last:
                                for k in range(4):
                                    kk = half * 4 + k
                                    for c in range(4):
                                        mm = pe.matmul(PS[c * 32:c * 32 + 32, b + 2 + m, 0:CTX],
                                                       at(xs + KT * CAP + kk * CAPC, CAPC),
                                                       w[:, k, c * CTX:c * CTX + CTX], start=(kk == 0), stop=(kk == KT - 1))
                            mm.then_inc(S("expert_used"), 1)
                    wt(pe, "hid", e + 1)
                    for c in range(4):
                        tr = pe.transpose(PS[:, b, c * P:c * P + P], at(hid + BW + c * P, P), ident)
                    if not last:
                        for c in range(2):
                            tr = pe.transpose(PS[:, b + 1, c * P:c * P + P], at(hid + 2 * BW + CTX + c * P, P), ident)
                    tr.then_inc(S("hid_turned"), 1)
                    wt(pe, "hid_taken", e + 1)
                    for half in range(2):
                        n = 4 + half
                        w = at(ES[n], SLOT).rearrange("p (k n) -> p k n", k=4)
                        pe.wait_ge(S(f"expert_in{n}"), e * 16 + (16 + base.get(f"expert_in{n}", 0)))
                        for k in range(4):
                            kk = half * 4 + k
                            for c in range(2):
                                mm = pe.matmul(PS[c * HD:c * HD + HD, b, :], at(hid + kk * CAP, CAP),
                                               w[:, k, c * BW:c * BW + BW], start=(kk == 0), stop=(kk == KT - 1))
                        if not last:
                            for k in range(4):
                                kk = half * 4 + k
                                for c in range(4):
                                    mm = pe.matmul(PS[c * 32:c * 32 + 32, b + 1, 0:CTX], at(hid + 2 * BW + kk * CAPC, CAPC),
                                                   w[:, k, c * CTX:c * CTX + CTX], start=(kk == 0), stop=(kk == KT - 1))
                        if half == 1:
                            mm.then_inc(S("ye_made"), 1)
                        else:
                            mm.then_inc(S("expert_used"), 1)
            for n, k in (("expert_used", 5), ("ye_made", 1), ("hid_turned", 1)):
                total[n] = total.get(n, 0) + k * N_EXP
            wt(pe, "ye", N_EXP + 2)
            for n in range(N_EXP // 2):
                wt(pe, "spread", n + 1)
                for i in range(KT):
                    mm = pe.matmul(PS[:, i, :], at(XIN + n * D + i * P, P), at(PTG + n % 3 * BW, BW),
                                   start=(n == 0), stop=(n == N_EXP // 2 - 1))
                inc(mm, "scattered")
            if not last:
                wt(pe, "moe_res", KT)
                wt(pe, "yc_stacked", 16)
                for n in range(N_EXP // 4):
                    m = N_EXP // 2 + n
                    wt(pe, "spread", m + 1)
                    for i in range(KT):
                        mm = pe.matmul(PS[:, i, 0:CTX], at(YCG + n * D + i * P, P), at(PTG + m % 3 * BW, CTX),
                                       start=(n == 0), stop=(n == N_EXP // 4 - 1))
                    inc(mm, "scattered")
            if last:
                ln_pe(pe, xq, nq, [(S("moe_res"), base.get("moe_res", 0) + KT)], center=False)
                pe.wait_ge(*ln_done(n_norm[0] + 2))
                for t in range(SEQ // P):
                    for half in range(2):
                        m = 2 * t + half
                        if m >= 4:
                            wt(pe, "final", m - 3)
                        for k in range(4):
                            tr = pe.transpose(PS[:, m % 4, k * P:k * P + P], at(hq(half * 4 + k) + t * P, P), ident)
                        inc(tr, "final_turned")

        @block.scalar
        def _(act):
            if l == 0:
                for k in range(KT):
                    wt(act, "ctx_turned", k + 1)
                    inc(nc.scalar.activation(at(xk(k), CTX), PS[:, 4 + k % 2, 0:CTX], ACT.Copy), "ctx_taken")
            sc = at(ASC, KT * 32).rearrange("p (k v) -> p k v", v=32)
            wt(act, "ada_zero", 1)
            inc(nc.scalar.activation(sc[:, :, 0], at(col["c"], KT), ACT.Silu), "ada_c")
            inc(nc.scalar.activation(sc[:, :, 1], at(col["c_ctx"], KT), ACT.Silu), "ada_c")

            def ada_free(n):
                if not isinstance(n, int) or n >= 2:
                    wt(act, "ada_turned", n - 1)
            take(act, f"ada{l}", lambda i, acc, j: nc.scalar.activation(mt[j], acc[:, 0, :], ACT.Copy), free=ada_free)
            def modulated(sg, sh, k, spans):
                for v, (c0, cn) in spans:
                    ins = nc.scalar.activation(at(hb(k) + c0, cn), at(hb(k) + c0, cn), ACT.Identity,
                                               bias=mod(sh, k, v), scale=at(sg + 2 * k + v, 1))
                return ins
            both = [(1, (0, CTX)), (0, (CTX, SEQ))]
            ln_act(act, xk, hb, T2, lambda k: modulated(SG1, 0, k, both), center=False,
                   pre=[(S("mod_ready"), base.get("mod_ready", 0) + 1)])
            q_at = lambda r: (lambda i, acc, j: nc.scalar.activation(
                spread(at(r + q0 + i * T2, nq), nqc), acc, ACT.Copy))
            k_at = lambda r: (lambda i, acc, j: nc.scalar.activation(spread(at(r + i * T2, T2), 2), acc, ACT.Copy))
            v_at = lambda i, acc, j: nc.scalar.activation(at(VR + i * BW, BW), acc[:, 0, :], ACT.Copy)
            take(act, f"u{l}", lambda i, acc, j: nc.scalar.activation(
                spread(at(YC + q0 + i * T2, nq), nqc), acc, ACT.Gelu_apprx_tanh))
            take(act, f"v{l}", lambda i, acc, j: nc.scalar.activation(at(VR + i * BW, BW), acc[:, 0, :], ACT.Gelu_apprx_tanh))
            wt(act, "ws_turned", 1)
            inc(nc.scalar.activation(at(WST, BW), PS[:, 4, :], ACT.Copy), "ws_taken")
            wt(act, "gm_var", 1)
            mv = at(GST, 2 * len(tok)).rearrange("p (t s) -> p t s", s=2)
            inc(nc.scalar.activation(mv[:, :, 1], mv[:, :, 1], ACT.Sqrt), "gm_sd")
            take(act, f"ka{l}", k_at(KR))
            take(act, f"va{l}", v_at)
            take(act, f"qa{l}", q_at(QR))
            wt(act, "rpb_turned", 1)
            inc(nc.scalar.activation(A[0:31, RPT:RPT + 120], PS[0:31, 4, 0:120], ACT.Copy), "rpb_taken")

            def attend(units, a, s_at, p_at, scale, ring):
                n_u, n_m = len(units), len(units[0]["maps"])
                seq_jobs, seq_units = counts(units)
                for n in range(n_u + 4):
                    if n < n_u:
                        for m in range(n_m):
                            j = n * n_m + m
                            wt(act, f"{a}_sc{j % 2}", j // 2 + 1)
                            if j >= ring:
                                old = (j - ring) // n_m
                                wt(act, f"{a}_t0", old + 1)
                                if seq_units[old]:
                                    wt(act, f"{a}_t1", seq_units[old])
                            inc(nc.scalar.activation(at(s_at(j), CTX), PS[:, j % 2 * 2, 0:CTX], ACT.Copy, scale=scale),
                                f"{a}_ctx{j % 2}")
                    if 1 <= n <= n_u:
                        for m in range(n_m):
                            j = (n - 1) * n_m + m
                            cell = CELLS + j % 8 * 3
                            wt(act, f"{a}_max", j + 1)
                            x = at(s_at(j), units[n - 1]["nk"] * P)
                            inc(nc.scalar.activation(x, x, ACT.Exp, bias=at(cell, 1), accum_out=at(cell + 1, 1)), f"{a}_e")
                    if 2 <= n <= n_u + 1:
                        u = units[n - 2]
                        w = min(u["nk"], 4) * P
                        wt(act, f"{a}_t0", n - 1)
                        if n >= 4:
                            wt(act, f"{a}_o", n - 3)
                        inc(nc.scalar.activation(at(p_at(n - 2), w), PS[:, 4, 0:w], ACT.Copy), f"{a}_pt0")
                    if n >= 4:
                        u = units[n - 4]
                        wt(act, f"{a}_o", n - 3)
                        inc(nc.scalar.activation(u["out"], PS[u["p0"]:u["p0"] + u["m"], 6 + (n - 1) % 2, 0:P], ACT.Copy),
                            f"{a}_out")

            attend(na, "na", NA_S, NA_P, NA_SCALE, 3)
            take(act, f"kb{l}", k_at(KR))
            take(act, f"vb{l}", v_at)
            take(act, f"qb{l}", q_at(QR))
            wt(act, "lam_dot", 1)
            inc(nc.scalar.activation(at(LAMS, 2), at(LAMS, 2), ACT.Exp), "lam_exp")
            attend(da, "da", DA_S, DA_P, DA_SCALE, 6)
            wt(act, "da_out", len(da))

            def sub_square(h):
                sq = at(SUB + h % 2 * T2, nq)
                wt(act, "sub_clip", h + 1)
                inc(nc.scalar.activation(sq, sq, ACT.Square), "sub_sq")

            def sub_beside(t):
                h = t // 2
                if t % 2 == 0:
                    wt(act, "sub_var", h + 1)
                    r = at(SUB + 2 * T2, nq)
                    inc(nc.scalar.activation(r, r, ACT.Sqrt, scale=ROOT_SCALE ** 2), "sub_sd")
                else:
                    wt(act, "sub_norm", h + 1)
                    y = at(YB + h * T2 + q0, nq)
                    inc(nc.scalar.activation(y, y, ACT.Identity, scale=at(SUBC, 1)), "sub_out")
                    if h + 1 < DA_H:
                        sub_square(h + 1)
            sub_square(0)
            for b in range(3):
                def gate_free(n):
                    if b:
                        wt(act, "merge", b * KT)
                take(act, f"gate{b}{l}", lambda i, acc, j: nc.scalar.activation(
                    spread(at(GATE + q0 + i * T2, nq), nqc), acc, ACT.Sigmoid), free=gate_free,
                    beside=None if b else sub_beside)
                s = st[f"branch{b}{l}"]
                for i in range(KT):
                    r = (s.tile0 + i) % 2
                    if b * KT + i >= 4:
                        wt(act, "merge", b * KT + i - 3)
                    act.wait_ge(S("acc_full"), s.tile0 + i + 1 + FULL0)
                    nc.scalar.activation(spread(at(PROD + i % 4 * T2, nq), nqc), PS[:, 2 * r:2 * r + nqc, 0:nq // nqc],
                                         ACT.Copy).then_inc(S("acc_free"), 1)
            take(act, f"out{l}", lambda i, acc, j: nc.scalar.activation(
                spread(at(GATE + q0 + i * T2, nq), nqc), acc, ACT.Copy), pre=[(S("merge"), base.get("merge", 0) + 3 * KT)])
            ln_act(act, xq, hq, nq, lambda k: modulated(SG2, 3, k, both if not last else both[1:]), center=False,
                   pre=[(S("attn_res"), base.get("attn_res", 0) + KT * (1 if last else 2))])
            wt(act, "logit_max", 1)
            aff = at(AFF, len(tok) * N_EXP)
            inc(nc.scalar.activation(aff, aff, ACT.Exp), "aff_exp")
            for m in range(2 * len(tok)):
                wt(act, "ht_turned", m + 1)
                inc(nc.scalar.activation(at(HT + m * BW, BW), PS[:, m % 4, :], ACT.Copy), "ht_taken")
            wt(act, "aff_turned", 1)
            n0 = min(4, len(tok)) * P
            nc.scalar.activation(A[0:N_EXP, AFT:AFT + n0], PS[0:N_EXP, 5, 0:n0], ACT.Copy).then_inc(S("aff_t0"), 1)
            if len(tok) > 4:
                nc.scalar.activation(A[0:N_EXP, AFT + n0:AFT + n0 + 2 * P], PS[0:N_EXP, 6, 0:2 * P], ACT.Copy)\
                    .then_inc(S("aff_t0"), 1)
            total["aff_t0"] = total.get("aff_t0", 0) + (2 if len(tok) > 4 else 1)
            wt(act, "col_turned", 1)
            nc_ = 2 * len(kinds) * N_EXP
            for n, (_, _, _, cap, dup) in enumerate(kinds):
                for q in range(dup):
                    r = slice(q * cap, q * cap + cap)
                    inc(nc.scalar.activation(A[r, ROWS + n * 8:ROWS + n * 8 + N_EXP // dup],
                                             PS[r, 4, 2 * n * N_EXP + q:(2 * n + 1) * N_EXP:dup], ACT.Copy), "rows")
            inc(nc.scalar.activation(at(COL, nc_), PS[:, 4, 0:nc_], ACT.Copy), "cols")
            xin = A[:, XIN:XIN + N_EXP * BW].rearrange("p (e k s) -> p e k s", k=KT, s=CAP)
            xinc = A[:, XINC:XINC + N_EXP * CTX].rearrange("p (e k s) -> p e k s", k=KT, s=CAPC)
            m = 0
            for k in range(KT):
                for half in range(2):
                    wt(act, "xin_made", m + 1)
                    inc(nc.scalar.activation(xin[:, 8 * half:8 * half + 8, k, :],
                                             PS[:, m % 4, :].rearrange("p (e s) -> p e s", s=CAP), ACT.Copy), "xin")
                    m += 1
                if not last:
                    wt(act, "xin_made", m + 1)
                    inc(nc.scalar.activation(xinc[:, :, k, :], PS[:, m % 4, :].rearrange("p (e s) -> p e s", s=CAPC), ACT.Copy),
                        "xin")
                    m += 1
            inc(act.nop(), "ye", 2)
            with act.Fori(0, N_EXP // 2) as e2:
                for u in range(2):
                    b, e, hid = 4 * u, e2 * 2 + u, HID[u]
                    wt(act, "expert_used", e * 5 + 4)
                    wt(act, "ye_made", e + 1)
                    ins = nc.scalar.activation(at(hid, BW), PS[:, b, :], ACT.Silu)
                    if not last:
                        ins = nc.scalar.activation(at(hid + 2 * BW, CTX), PS[:, b + 2, 0:CTX], ACT.Silu)
                    ins.then_inc(S("silu"), 1)
                    wt(act, "hid_turned", e + 1)
                    ins = nc.scalar.activation(
                        at(hid, BW).rearrange("p (h c s) -> p c h s", h=2, s=CAP),
                        PS[:, b, :].rearrange("p (c h s) -> p c h s", c=4, h=2), ACT.Copy)
                    if not last:
                        ins = nc.scalar.activation(
                            at(hid + 2 * BW, CTX).rearrange("p (q c s) -> p c q s", q=4, s=CAPC),
                            PS[:, b + 1, 0:CTX].rearrange("p (c q s) -> p c q s", c=2, q=4), ACT.Copy)
                    ins.then_inc(S("hid_taken"), 1)
                    wt(act, "ye_made", e + 3)
                    if u == 0:
                        wt(act, "xs", e + 2)
                    gate = e + (COL + N_EXP)
                    for c in range(2):
                        r = slice(c * HD, c * HD + HD)
                        ins = nc.scalar.activation(at(e2 * D + (XIN + c * BW), BW, u * HD, u * HD + HD), PS[r, b, :], ACT.Copy,
                                                   scale=at(gate, 1, c * HD, c * HD + HD))
                    if not last:
                        ins = nc.scalar.activation(at(e * CTX + XINC, CTX), PS[:, b + 1, 0:CTX], ACT.Copy,
                                                   scale=at(gate + 2 * N_EXP, 1))
                    ins.then_inc(S("ye"), 1)
            for n, k in (("silu", 1), ("hid_taken", 1), ("ye", 1)):
                total[n] = total.get(n, 0) + N_EXP
            if not last:
                wt(act, "ye", N_EXP + 2)
                wt(act, "ye_made", N_EXP + 2)
                for q in range(4):
                    for c in range(4):
                        src = A[c * 32:c * 32 + 32, XINC:XINC + N_EXP * CTX].rearrange("p (g q s) -> p g q s", q=4, s=CTX)
                        dst = A[q * 32:q * 32 + 32, YCG:YCG + 4 * D].rearrange("p (g c s) -> p g c s", c=4, s=CTX)
                        inc(nc.scalar.activation(dst[:, :, c, :], src[:, :, q, :], ACT.Copy), "yc_stacked")
            if last:
                ln_act(act, xq, hq, nq, lambda k: nc.scalar.activation(at(hq(k), nq), at(hq(k), nq), ACT.Identity,
                                                                       scale=pc("g_final", k)), center=False,
                       pre=[(S("moe_res"), base.get("moe_res", 0) + KT)])
                for m in range(2 * SEQ // P):
                    wt(act, "final_turned", m + 1)
                    inc(nc.scalar.activation(at(HT + m * BW, BW), PS[:, m % 4, :], ACT.Copy), "final")

        @block.gpsimd
        def _(pool):
            wt(pool, "na_over", 1)
            inc(pool.dma_start(at(COS, 2 * SEQ), I["const2"][:, N_CONST2:]), "rope_in", 16)
            wt(pool, "gathered", 1)
            with pool.Fori(0, N_EXP // 2) as e2:
                for u in range(2):
                    e, xs = e2 * 2 + u, HID[u] + 3 * BW
                    wt(pool, "ye_made", e + 1)
                    ins = nc.gpsimd.tensor_copy(at(xs, BW), at(e * BW + XIN, BW))
                    if not last:
                        ins.then_inc(S("xs0"), 1)
                        ins = nc.gpsimd.tensor_copy(at(xs + BW, CTX), at(e * CTX + XINC, CTX))
                    ins.then_inc(S("xs"), 1)
            total["xs"] = total.get("xs", 0) + N_EXP

        @block.vector
        def _(dve):
            V = nc.vector
            step = Step(dve, S("dve_step"))
            step.n = dve_steps[0]
            if l == 0:
                wt(dve, "const2_in", 16)
            inc(V.memset(at(ASC, KT * 32), 0.0), "ada_zero")
            bias = col[f"b_ada{l}"]

            def ada_one(n, u):
                wt(dve, "ada_turned", n + 1)
                V.tensor_tensor(at(n * 8 + MOD, 8).rearrange("p (q v) -> p q v", v=2),
                                PS[:, 4 + u, 0:P].rearrange("p (q r) -> p q r", r=32)[:, :, 0:2],
                                at(n * 4 + bias, 4).unsqueeze(2).to_broadcast([P, 4, 2]), ALU.add).then_inc(S("ada_mod"), 1)
            loop(dve, s_ada.slabs, ada_one)
            total["ada_mod"] = total.get("ada_mod", 0) + s_ada.slabs
            wt(dve, "ada_mod", s_ada.slabs)
            for sg, m, g in ((SG1, 1, "g_norm1"), (SG2, 4, "g_norm2")):
                step(V.scalar_tensor_tensor(
                    out=at(sg, KT * 2).rearrange("p (k v) -> p k v", v=2), in0=mod8(m), scalar=1.0,
                    in1=at(col[f"{g}{l}"], KT).unsqueeze(2).to_broadcast([P, KT, 2]), op0=ALU.add, op1=ALU.mult))
            lam_init = 0.8 - 0.6 * float(np.exp(-0.3 * l))
            step(V.tensor_scalar(at(SUBC, 1), pc(f"subln{l}"), 1.0 - lam_init, ROOT_SCALE, ALU.mult, ALU.mult))
            step.done()
            if l == 0:
                wt(dve, "ctx_taken", KT)
            inc(dve.nop(), "mod_ready")
            ln_dve(dve, step, xk, hb, T2, RMS_EPS, center=False)
            wt(dve, "small_in", 16 * n_small)
            nt = len(tok)
            stats = at(SCR + 5 * BW, 6 * nt)
            mv = at(GST, 2 * nt).rearrange("p (t s) -> p t s", s=2)
            for n in range(nt):
                dve.wait_ge(*taken(f"v{l}", n + 1))
                step(V.bn_stats(stats[:, 6 * n:6 * n + 6], at(VR + n * BW, BW)))
            step.done()
            for n in range(nt):
                step(V.bn_aggr(mv[:, n, :], stats[:, 6 * n:6 * n + 6]))
            step.done()
            inc(V.tensor_scalar(mv[:, :, 1], mv[:, :, 1], RMS_EPS, None, ALU.add), "gm_var")
            wt(dve, "gm_sd", 1)
            step(V.reciprocal(mv[:, :, 1], mv[:, :, 1]))
            step.done()
            for n in range(nt):
                v = at(VR + n * BW, BW)
                step(V.tensor_scalar(v, v, mv[:, n, 0:1], mv[:, n, 1:2], ALU.subtract, ALU.mult))
            step.done()
            for n in range(nt):
                v = at(VR + n * BW, BW)
                step(V.tensor_tensor(v, v, at(GMG, BW), ALU.mult))
            step.done()
            for n in range(nt):
                v = at(VR + n * BW, BW)
                inc(V.tensor_tensor(v, v, at(GMB, BW), ALU.add), "gm_normed")
            for g in range(4):
                wt(dve, "gm_mixed", g + 1)
                mixed = at(SCR + 6 * BW, nt * P).rearrange("p (n t) -> p n t", t=P)
                for b in range(-(-nt // 4)):
                    m = min(4, nt - 4 * b)
                    step(V.tensor_tensor(mixed[:, 4 * b:4 * b + m, :],
                                         PS[:, 4 + g % 2 * 2 + b, 0:m * P].rearrange("p (n t) -> p n t", t=P),
                                         at(BSR + g * P, P).unsqueeze(1).to_broadcast([P, m, P]), ALU.add))
                step.done()
                dve.wait_ge(*taken(f"u{l}"))
                y = at(YC + g * T2 + q0, nq)
                inc(V.tensor_tensor(y, y, at(SCR + 6 * BW, nq), ALU.mult), "gm_done")
                wt(dve, "gm_done", g + 1)
            for n in range(2):
                prod = at(LAM + 2 * n * HD, HD)
                step(V.tensor_tensor(prod, prod, at(LAM + (2 * n + 1) * HD, HD), ALU.mult))
            step.done()
            ins = V.tensor_reduce(at(LAMS, 2), at(LAM, 4 * HD).rearrange("p (n m c) -> p n m c", m=2, c=HD)[:, :, 0, :],
                                  AX.X, ALU.add)
            inc(ins, "lam_dot")
            for c4 in range(GRID_W // 4):
                wt(dve, "bias_made", c4 + 1)
                src = PS[:, 4 + c4 % 4, 0:480].rearrange("p (c h r) -> p h r c", c=4, h=NA_H)
                for p0 in (0, HD):
                    r = slice(p0, p0 + HD)
                    for half in range(2):
                        j = 1 if p0 else 0
                        inc(V.tensor_tensor(
                            bm[half][r, :, j:j + 15, c4 * 4:c4 * 4 + 4],
                            src[r, half * half_bm:(half + 1) * half_bm],
                            A[r, WIN + c4 * 4:WIN + c4 * 4 + 4].unsqueeze(1).unsqueeze(1).to_broadcast([HD, half_bm, 15, 4]),
                            ALU.add), "bias_taken")
            wt(dve, "bias_taken", 4 * (GRID_W // 4))

            def attend(units, a, s_at, p_at, scale, ring):
                n_u, n_m = len(units), len(units[0]["maps"])
                seq_jobs, seq_units = counts(units)
                for n in range(n_u + 2):
                    if n < n_u:
                        u = units[n]
                        for m in range(n_m):
                            j = n * n_m + m
                            cell = CELLS + j % 8 * 3
                            if j >= ring:
                                old = (j - ring) // n_m
                                wt(dve, f"{a}_t0", old + 1)
                                if seq_units[old]:
                                    wt(dve, f"{a}_t1", seq_units[old])
                            if u["nk"] > 2:
                                wt(dve, f"{a}_ss{j % 2}", seq_jobs[j])
                                x, acc = at(s_at(j) + CTX, SEQ), PS[:, j % 2 * 2 + 1, :]
                                if u["bias"]:
                                    h, j0 = u["bias"]
                                    b = bm[h // half_bm][:, h % half_bm, j0:j0 + WIN_R, :]
                                    ins = V.scalar_tensor_tensor(
                                        out=x.rearrange("p (r c) -> p r c", c=GRID_W),
                                        in0=acc.rearrange("p (r c) -> p r c", c=GRID_W),
                                        scalar=scale, in1=b, op0=ALU.mult, op1=ALU.add)
                                else:
                                    ins = V.tensor_scalar(x, acc, scale, None, ALU.mult)
                                inc(ins, f"{a}_seq{j % 2}")
                                wt(dve, f"{a}_seq{j % 2}", seq_jobs[j])
                            wt(dve, f"{a}_ctx{j % 2}", j // 2 + 1)
                            if j >= 8:
                                wt(dve, f"{a}_e", j - 7)
                            inc(V.tensor_reduce(at(cell, 1), at(s_at(j), u["nk"] * P), AX.X, ALU.max, negate=True), f"{a}_max")
                    if 1 <= n <= n_u:
                        u = units[n - 1]
                        w = u["nk"] * P
                        j = (n - 1) * n_m
                        cells = [CELLS + (j + m) % 8 * 3 for m in range(n_m)]
                        wt(dve, f"{a}_e", j + n_m)
                        for c in cells:
                            step(V.reciprocal(at(c + 2, 1), at(c + 1, 1)))
                        step.done()
                        x = at(s_at(j), w)
                        if n_m == 1:
                            inc(V.tensor_scalar(x, x, at(cells[0] + 2, 1), None, ALU.mult), f"{a}_p")
                        else:
                            x1 = at(s_at(j + 1), w)
                            step(V.tensor_scalar(x1, x1, at(cells[1] + 2, 1), at(LAMC, 1), ALU.mult, ALU.mult))
                            step.done()
                            inc(V.scalar_tensor_tensor(out=x, in0=x, scalar=at(cells[0] + 2, 1), in1=x1,
                                                       op0=ALU.mult, op1=ALU.subtract), f"{a}_p")
                    if n >= 2 and units[n - 2]["nk"] > 4:
                        wt(dve, f"{a}_t1", seq_units[n - 2])
                        if n >= 4:
                            wt(dve, f"{a}_o", n - 3)
                        inc(V.tensor_copy(at(p_at(n - 2) + 4 * P, 2 * P), PS[:, 5, 0:2 * P]), f"{a}_pt1")

            attend(na, "na", NA_S, NA_P, NA_SCALE, 3)
            wt(dve, "na_p", len(na))
            inc(dve.nop(), "na_over")
            wt(dve, "lam_exp", 1)
            step(V.tensor_scalar(at(LAMC, 1), at(LAMS, 1), at(LAMS + 1, 1), lam_init, ALU.subtract, ALU.add))
            wt(dve, "rope_in", 16)
            for n in range(8):
                r = at((KR if n < 4 else QR) + n % 4 * T2 + CTX, SEQ)
                t = at(SCR + n % 4 * SEQ, SEQ)
                wt(dve, "rope_r", n + 1)
                inc(V.tensor_tensor(t, PS[:, 4 + n % 4, :], at(SIN, SEQ), ALU.mult), "rope_t")
                step(V.tensor_tensor(r, r, at(COS, SEQ), ALU.mult))
                step.done()
                wt(dve, "rope_t", n + 1)
                inc(V.tensor_tensor(r, r, t, ALU.add), "rope_done")
            wt(dve, "rope_done", 8)
            attend(da, "da", DA_S, DA_P, DA_SCALE, 6)
            wt(dve, "da_out", len(da))

            def clip(h):
                inc(V.tensor_scalar(at(SUB + h % 2 * T2, nq), at(YB + h * T2 + q0, nq), SQ_MAX, -SQ_MAX, ALU.min, ALU.max),
                    "sub_clip")
            clip(0)
            for h in range(DA_H):
                if h + 1 < DA_H:
                    if h:
                        wt(dve, "sub_sum", h)
                    clip(h + 1)
                wt(dve, "sub_sum", h + 1)
                r = at(SUB + 2 * T2, nq)
                inc(V.tensor_scalar(halves(r), PS[:, 4 + h % 2 * 2:6 + h % 2 * 2, 0:nq // 2], RMS_EPS, None, ALU.add), "sub_var")
                wt(dve, "sub_sd", h + 1)
                step(V.reciprocal(r, r))
                step.done()
                mean = PS[:, 4 + h % 2 * 2:6 + h % 2 * 2, 0:nq // 2]
                inc(V.scalar_tensor_tensor(out=halves(r), in0=mean, scalar=MEAN_MAX, in1=halves(r),
                                           op0=ALU.is_lt, op1=ALU.mult), "sub_rstd")
                wt(dve, "sub_rstd", h + 1)
                y = at(YB + h * T2 + q0, nq)
                inc(V.tensor_tensor(y, y, r, ALU.mult), "sub_norm")
                wt(dve, "sub_norm", h + 1)
            for b in range(3):
                s = st[f"branch{b}{l}"]
                for i in range(KT):
                    dve.wait_ge(*taken(f"branch{b}{l}", i + 1))
                    pr, gt, m = (at(o + q0, nq) for o in (PROD + i % 4 * T2 - q0, GATE + i * T2, MERGED + i * T2))
                    if b == 0:
                        inc(V.tensor_tensor(m, pr, gt, ALU.mult), "merge")
                    else:
                        step(V.tensor_tensor(pr, pr, gt, ALU.mult))
                        step.done()
                        wt(dve, "merge", (b - 1) * KT + i + 1)
                        inc(V.tensor_tensor(m, m, pr, ALU.add), "merge")
            spans = [(0, CTX, SEQ)] + ([] if last else [(1, 0, CTX)])
            for i in range(KT):
                dve.wait_ge(*taken(f"out{l}", i + 1))
                for v, c0, cn in spans:
                    x = at(xk(i) + c0, cn)
                    ins = V.scalar_tensor_tensor(out=x, in0=at(GATE + i * T2 + c0, cn), scalar=mod(2, i, v), in1=x,
                                                 op0=ALU.mult, op1=ALU.add)
                    inc(ins, "attn_res")
            wt(dve, "attn_res", KT * len(spans))
            ln_dve(dve, step, xq, hq, nq, RMS_EPS, center=False)
            wt(dve, "logits", 1)
            aff = at(AFF, nt * N_EXP).rearrange("p (t e) -> p t e", e=N_EXP)
            mx = at(WRK, nt)
            step(V.tensor_reduce(mx, PS[:, 4, 0:nt * N_EXP].rearrange("p (t e) -> p t e", e=N_EXP), AX.X, ALU.max))
            step.done()
            inc(V.tensor_tensor(aff, PS[:, 4, 0:nt * N_EXP].rearrange("p (t e) -> p t e", e=N_EXP),
                                mx.unsqueeze(2).to_broadcast([P, nt, N_EXP]), ALU.subtract), "logit_max")
            wt(dve, "aff_exp", 1)
            step(V.tensor_reduce(mx, aff, AX.X, ALU.add))
            step.done()
            step(V.reciprocal(mx, mx))
            step.done()
            inc(V.tensor_tensor(aff, aff, mx.unsqueeze(2).to_broadcast([P, nt, N_EXP]), ALU.mult), "aff")
            wt(dve, "aff_t0", 2 if nt > 4 else 1)
            e16 = lambda o, n: A[0:N_EXP, o:o + n]
            val, idx = e16(VAL, CAP + CAPC), e16(IDX, CAP + CAPC).bitcast(U32)
            for n, (_, c0, cn, cap, dup) in enumerate(kinds):
                work = e16(WRK + n * SEQ, cn)
                step(V.tensor_copy(work, e16(AFT + c0 - q0, cn)))
                step.done()
                for r in range(cap // 8):
                    o = n * CAP + r * 8
                    step(V.max(val[:, o:o + 8], work))
                    step.done()
                    step(V.max_index(idx[:, o:o + 8], val[:, o:o + 8], work))
                    step.done()
                    step(V.match_replace(work, val[:, o:o + 8], work, -1.0))
                    step.done()
                o = n * CAP
                for d in range(dup):
                    step(V.tensor_copy(e16(IDF + n * P + d * cap, cap), idx[:, o:o + cap]))
                    step(V.tensor_copy(e16(GTF + n * P + d * cap, cap), val[:, o:o + cap]))
            step.done()
            inc(dve.nop(), "chosen")
            wt(dve, "idx_in", 16 * len(kinds))
            for t in range(SEQ // P):
                inc(V.tensor_scalar(at(PG + t * D, D), at(IB, D), at(CNT + t, 1), None, ALU.is_equal), "onehot")
            if not last:
                for t in range(CTX // P):
                    inc(V.tensor_scalar(at(PGC + t * BW, BW), at(IB + D, BW), at(CNT + t, 1), None, ALU.is_equal), "onehot")
            wt(dve, "gathered", 1)
            with dve.Fori(0, N_EXP // 2) as e2:
                for u in range(2):
                    b, e, hid = 4 * u, e2 * 2 + u, HID[u]
                    wt(dve, "silu", e + 1)
                    wt(dve, "expert_used", e * 5 + 4)
                    ins = V.tensor_tensor(at(hid + BW, BW), at(hid, BW), PS[:, b + 1, :], ALU.mult)
                    if not last:
                        ins = V.tensor_tensor(at(hid + 2 * BW + CTX, CTX), at(hid + 2 * BW, CTX), PS[:, b + 3, 0:CTX], ALU.mult)
                    ins.then_inc(S("hid"), 1)
            total["hid"] = total.get("hid", 0) + N_EXP
            wt(dve, "rows", sum(k[4] for k in kinds))
            wt(dve, "ye_made", N_EXP + 2)
            n = 0
            for kind, (_, c0, cn, cap, dup) in enumerate(kinds):
                for m in range(N_EXP // dup):
                    if n >= 3:
                        wt(dve, "scattered", n - 2)
                    inc(V.tensor_scalar(at(PTG + n % 3 * BW, cn), at(TOK, cn), at(ROWS + kind * 8 + m, 1), None, ALU.is_equal),
                        "spread")
                    n += 1
                wt(dve, "scattered", n)
                for i in range(KT):
                    x = at(xk(i) + c0, cn)
                    inc(V.scalar_tensor_tensor(out=x, in0=PS[:, i, 0:cn], scalar=mod(5, i, kind), in1=x,
                                               op0=ALU.mult, op1=ALU.add), "moe_res")
            if last:
                wt(dve, "moe_res", KT)
                ln_dve(dve, step, xq, hq, nq, RMS_EPS, center=False)
            dve_steps[0] = step.n

        block.__exit__(None, None, None)

    hk = lambda k: H + k * T1
    ck = lambda k: CS + k * T1
    AW = CONV_K - 1 + T1
    ak = lambda k: A_ + k * AW
    rhs_h = lambda k, c0, cn: at(H + k * T1 + c0, cn)
    XS = R_
    XM = R_ + 4 * D
    PST = V_
    LW = T1 + 1
    t_ = [TMP + n * T1 for n in range(8)]
    FREE = RING + (1 - st["lora_up"].slot0) * SLOT
    sig = [(t_[0], t_[1]), (FREE, FREE + T1)]
    kn = FREE + 2 * T1

    W_AT, W_X, W_XT, W_Y, W_AL = (RING + n * 1024 for n in range(5))
    W_MS, W_BK_IN = RING + 5120, RING + 7168
    W_RAV, W_BK, W_UV, W_W, W_G = TMP, TMP + 1536, TMP + 2560, TMP + 3584, TMP + 4096
    bk_in = sb(W_BK_IN, KT * P).rearrange("p (i t) -> p i t", i=KT)
    rav = sb(W_RAV, KT * 3 * CH).rearrange("p (i t) -> p i t", i=KT)
    bk, uv, ms = sb(W_BK, HEADS * HD), sb(W_UV, HEADS * HD), sb(W_MS, HEADS * P)
    pairs = lambda off: sb(off, KT * P).rearrange("p (i t) -> p i t", i=KT)
    at_m, x_m, xt_m, y_m, al_m = (pairs(o) for o in (W_AT, W_X, W_XT, W_Y, W_AL))
    w_v = sb(W_W, KT * HD)
    g_v = sb(W_G, KT * HD)
    JOINS = LEVELS - 1
    mc = lambda h: (h % 2 * KT + h // 2) * P
    UB, UW, FC, F_ = R_, T1 + FFN_K - 1, B_, K_

    def in_chunk(off, c):
        return A[:, off:off + KT * TP].rearrange("p (i t) -> p i t", t=TP)[:, :, ds(c * CH, CH)]

    block = nc.Block()
    block.__enter__()

    @block.sync
    def _(sp):
        sp.dma_start(A[:, IDN:IDN + N_CONST], I["const1"]).then_inc(S("const_in"), 16)
        sp.wait_ge(S("rows_zero"), 1)
        for r0, ap, n in dram_rows:
            done = 0
            while done < n:
                p0, t = (r0 + done) % P, (r0 + done) // P
                m = min(n - done, P - p0)
                sp.dma_start(A[p0:p0 + m, PST + t * P:PST + t * P + ap.shape[-1]], ap[done:done + m, :])\
                    .then_inc(S("rows_in"), 16)
                done += m
        sp.dma_start(A[0:N_META, XM:XM + D], I["meta_tokens"]).then_inc(S("x_in"), 16)
        sp.dma_start(A[:, XS:XS + 4 * D].rearrange("p (t c) -> p t c", t=4),
                     I["x"][0].rearrange("(t p) c -> p t c", p=P)).then_inc(S("x_in"), 16)

        def slabs(w, first):
            wv = w.rearrange("(k p) n -> p k n", p=P)

            def src(n, dst):
                c0 = n * (4 * P) + first
                ap = wv[:, :, c0:c0 + 4 * P] if isinstance(n, int) else wv[:, :, ds(c0, 4 * P)]
                return [(dst[:, 0:KT * 4 * P].rearrange("p (k n) -> p k n", k=KT), ap)]
            return src

        w_in = I["w_in"][0]
        stream(sp, "glu_a", slabs(w_in, 0))
        stream(sp, "glu_g", slabs(w_in, D))
        stream(sp, "rkv", slabs(w_in, 2 * D))
        n_lora = 288
        stream(sp, "lora", lambda n, dst: [(
            dst[:, 0:KT * 384].rearrange("p (k n) -> p k n", k=KT)[:, :, 0:n_lora],
            w_in.rearrange("(k p) n -> p k n", p=P)[:, :, 5 * D:5 * D + n_lora])])
        stream(sp, "lora_up", lambda n, dst: [(dst[0:HD, 0:D], I["w_decay_up"][0]), (dst[HD:P, 0:D], I["a_up"][0])])
        stream(sp, "g_up", lambda n, dst: [
            (dst[:, 0:D], I["g_up"][0][0:P, :]), (dst[0:32, D:2 * D], I["g_up"][0][P:, :])],
            pre=[(S("prep_done"), KT), (S("wk_state"), NCH + 1), (S("wk_out"), NCH + 1)])
        stream(sp, "gates", slabs(w_in, 2 * D + 3360))
        stream(sp, "conv_out", slabs(I["w_conv_out"][0], 0))
        stream(sp, "rwkv_out", slabs(I["w_rwkv_out"][0], 0))
        stream(sp, "w_o", slabs(I["w_o"][0], 0))
        up = I["ffn_up"][0].rearrange("(k p) n -> p k n", p=P)

        def ffn_src(n, dst):
            dst = dst.rearrange("p (k h n) -> p k h n", k=KT, h=2)
            cut = lambda c0: up[:, :, c0:c0 + 2 * P] if isinstance(n, int) else up[:, :, ds(c0, 2 * P)]
            return [(dst[:, :, h, :], cut(n * (2 * P) + h * D_FF)) for h in range(2)]
        stream(sp, "ffn_up", ffn_src)
        down = I["ffn_down"][0].rearrange("(k p) n -> p k n", p=P)
        stream(sp, "ffn_down", lambda n, dst: [(
            dst[:, 0:FT * P].rearrange("p (k n) -> p k n", k=FT),
            down[:, :, n * P:n * P + P] if isinstance(n, int) else down[:, :, ds(n * P, P)])])

    def count_rows():
        n_dma = 0
        for r0, ap, n in dram_rows:
            n_dma += (r0 + n - 1) // P - r0 // P + 1
        return 16 * n_dma

    @block.tensor
    def _(pe):
        pe.nop().then_inc(S("acc_full"), FULL0)
        pe.wait_ge(S("const_in"), 16)
        pe.wait_ge(S("rows_in"), count_rows())
        for t in range(n_par):
            tr = pe.transpose(PS[:, t // 4, t % 4 * P:t % 4 * P + P], sb(PST + t * P, P), ident)
        tr.then_inc(S("rows_turned"), 1)
        pe.wait_ge(S("x_in"), 32)
        for k in range(KT):
            b = 2 + k % 2 * 2
            if k >= 2:
                pe.wait_ge(S("x_taken"), 2 * k - 2)
            for t in range(4):
                pe.transpose(PS[:, b, t * P:t * P + P], sb(XS + t * D + k * P, P), ident)
            pe.transpose(PS[:, b + 1, 0:N_META], A[0:N_META, XM + k * P:XM + k * P + P], ident[0:N_META, 0:N_META])\
                .then_inc(S("x_turned"), 1)
        ln_pe(pe, hk, T1, [(S("x_taken"), 2 * KT), (S("par_ready"), 1)])
        products(pe, "glu_a", rhs_h, first=ln_tile(0))
        products(pe, "glu_g", rhs_h)
        products(pe, "rkv", rhs_h)
        products(pe, "lora", rhs_h, width=[P, P, 32])
        ln_pe(pe, ck, T1, [(S("conv"), KT * CONV_K)])
        s = st["lora_up"]
        pe.wait_ge(S(f"w_in{s.slot0}"), 16 * (s.used0[s.slot0] + s.dmas))
        pe.wait_ge(S("lora_act"), 3)
        pe.wait_ge(*taken("lora"))
        up = slot[s.slot0]

        def prep_up(i):
            if i:
                pe.wait_ge(S("prep_sig"), 2 * i)
            for p0, b in ((0, 0), (HD, 2)):
                for c in range(2):
                    mm = pe.matmul(PS[:, b + c, 0:C1], up[p0:p0 + HD, i * P:i * P + P],
                                   A[p0:p0 + HD, LO + 1 + c * C1:LO + 1 + c * C1 + C1], start=True, stop=True)
                mm.then_inc(S("prep_up"), 1)
        prep_up(0)
        for i in range(KT):
            if i + 1 < KT:
                prep_up(i + 1)
            if i:
                pe.wait_ge(S("prep_done"), i)
            pe.wait_ge(S("prep_kk"), i + 1)
            for c in range(2):
                mm = pe.matmul(PS[:, 4 + c, 0:C1], ones_h, at(t_[7] + c * C1, C1), start=True, stop=True)
            mm.then_inc(S("prep_ss"), 1)
            pe.wait_ge(S("prep_rk"), i + 1)
            for c in range(2):
                mm = pe.matmul(PS[:, 6 + c, 0:C1], ones_h, at(sig[i % 2][0] + c * C1, C1), start=True, stop=True)
            mm.then_inc(S("prep_bs"), 1)
        pe.wait_ge(S("prep_done"), KT)
        with pe.Fori(0, NCH) as c:
            pe.wait_ge(S("wk_bk_in"), c * 2 + 2)
            pe.wait_ge(S("wk_ra_in"), c * 2 + 2)
            pe.wait_ge(S("wk_g"), c + 1)
            pe.wait_ge(S("wk_out"), c + 1)
            for n in range(HEADS):
                p0, i = n // KT * HD, n % KT
                mm = pe.matmul(PS[:, n // 4, n % 4 * P:n % 4 * P + P], bk_in[p0:p0 + HD, i, :],
                               rav[p0:p0 + HD, i, 0:2 * CH], start=True, stop=True)
                if n % 4 == 3:
                    mm.then_inc(S("wk_scores"), 1)
            for i in range(KT):
                mm = pe.transpose(PS[:, 4 + i // 4, i % 4 * P:i % 4 * P + P], bk_in[:, i, :], ident)
            mm.then_inc(S("wk_turned"), 1)
            pe.wait_ge(S("wk_v_in"), c + 1)
            for i in range(KT):
                mm = pe.transpose(PS[:, 6 + i // 4, i % 4 * P:i % 4 * P + P], rav[:, i, CH:3 * CH], ident)
            mm.then_inc(S("wk_turned"), 1)
            pe.wait_ge(S("wk_xt0"), c + 1)
            pe.wait_ge(S("wk_masked"), c * 4 + 4)
            for i in range(KT):
                mm = pe.transpose(PS[:, i // 4, i % 4 * P:i % 4 * P + P], xt_m[:, i, :], ident)
            mm.then_inc(S("wk_x0"), 1)
            for level in range(JOINS):
                for q in range(2):
                    if level == 0:
                        pe.wait_ge(S("wk_x0_out"), c + 1)
                        pe.wait_ge(S("wk_bk"), c * 2 + 2)
                    else:
                        pe.wait_ge(S("wk_joined"), c * (4 * JOINS - 2) + 4 * (level - 1) + 2 * q + 2)
                    pe.wait_ge(S("wk_al"), c * JOINS + level + 1)
                    for i in range(4 * q, 4 * q + 4):
                        mm = pe.matmul(PS[:, 4 + q, i % 4 * P:i % 4 * P + P], al_m[:, i, :], x_m[:, i, :],
                                       start=True, stop=True)
                    mm.then_inc(S("wk_y"), 1)
                if level == 0:
                    pe.wait_ge(S("wk_state"), c + 1)
                    pe.nop().then_inc(S("wk_state_seen"), 1)
                    for h in range(HEADS):
                        p0, i = h % 2 * HD, h // 2
                        pe.matmul(PS[p0:p0 + HD, 2, i * HD:i * HD + HD], rav[p0:p0 + HD, i, CH:2 * CH],
                                  g_v[p0:p0 + HD, i * HD:i * HD + HD], start=True, stop=True)
                        mm = pe.matmul(PS[p0:p0 + HD, 3, i * HD:i * HD + HD], ms[HD:P, mc(h) + CH:mc(h) + 2 * CH],
                                       uv[HD:P, h * HD:h * HD + HD], start=True, stop=True)
                    mm.then_inc(S("wk_w"), 1)
                for q in range(2):
                    pe.wait_ge(S("wk_y_out"), c * (2 * JOINS) + 2 * level + q + 1)
                    for i in range(4 * q, 4 * q + 4):
                        mm = pe.matmul(PS[:, 6 + q, i % 4 * P:i % 4 * P + P], y_m[:, i, :], xt_m[:, i, :],
                                       start=True, stop=True)
                        if level < JOINS - 1:
                            mm = pe.matmul(PS[:, q, i % 4 * P:i % 4 * P + P], xt_m[:, i, :], y_m[:, i, :],
                                           start=True, stop=True)
                    mm.then_inc(S("wk_join"), 1)
            pe.wait_ge(S("wk_joined"), c * (4 * JOINS - 2) + 4 * JOINS - 2)
            pe.wait_ge(S("wk_w_out"), c + 1)
            for i in range(KT):
                mm = pe.matmul(PS[:, 3, i * HD:i * HD + HD], xt_m[:, i, :], w_v[:, i * HD:i * HD + HD],
                               start=True, stop=True)
            mm.then_inc(S("wk_u"), 1)
            pe.wait_ge(S("wk_u_out"), c * 2 + 2)
            for h in range(HEADS):
                p0, i = h % 2 * HD, h // 2
                pe.matmul(PS[p0:p0 + HD, 0, i * HD:i * HD + HD], bk[:, h * HD:h * HD + HD],
                          uv[:, h * HD:h * HD + HD], start=True, stop=True)
            for h in range(HEADS):
                p0, i = h % 2 * HD, h // 2
                o = PS[p0:p0 + HD, 1, i * CH:i * CH + CH]
                pe.matmul(o, g_v[p0:p0 + HD, i * HD:i * HD + HD], rav[p0:p0 + HD, i, 0:CH], start=True, stop=False)
                mm = pe.matmul(o, uv[:, h * HD:h * HD + HD], ms[:, mc(h):mc(h) + CH], start=False, stop=True)
            mm.then_inc(S("wk_end"), 1)
        pe.wait_ge(S("wk_out"), NCH + 1)
        pe.wait_ge(S("wk_state"), NCH + 1)
        products(pe, "g_up", lambda k, c0, cn: at(LO + (k + 1) * LW + 1 + c0, cn, 0, (P, 32)[k]), depth=(P, 32))

        def gn_beside(t):
            i, y = t // 2, R_ + t // 2 * TP + PADT
            if t % 2 == 0:
                if i:
                    pe.wait_ge(S("gn_cent"), i)
                for c in range(2):
                    mm = pe.matmul(PS[:, 4 + c, 0:C1], mean_h, at(y + c * C1, C1), start=True, stop=True)
                mm.then_inc(S("gn_sum"), 1)
            else:
                pe.wait_ge(S("gn_sq"), i + 1)
                if i:
                    pe.wait_ge(S("gn_var"), i)
                for c in range(2):
                    mm = pe.matmul(PS[:, 6 + c, 0:C1], mean_h, at(SQ + i % 2 * T1 + c * C1, C1), start=True, stop=True)
                mm.then_inc(S("gn_sum2"), 1)
        products(pe, "gates", rhs_h, beside=gn_beside)
        products(pe, "conv_out", lambda k, c0, cn: at(CS + k * T1 + c0, cn))
        products(pe, "rwkv_out", lambda k, c0, cn: at(R_ + k * TP + PADT + c0, cn), [(S("gn_o"), KT)])
        products(pe, "w_o", lambda k, c0, cn: at(B_ + k * T1 + c0, cn), first=lambda k: (S("merged"), k + 1))
        ln_pe(pe, hk, T1, [(S("res1"), KT)])
        products(pe, "ffn_up", rhs_h, first=ln_tile(2))
        products(pe, "ffn_down", lambda k, c0, cn: at(F_ + k * T1 + c0, cn), [(S("ffn_f"), FT)])
        ln_pe(pe, hk, T1, [(S("res2"), KT)])

    @block.scalar
    def _(act):
        act.nop().then_inc(S("acc_free"), FREE0)
        act.wait_ge(S("rows_turned"), 1)
        n0 = min(n_par, 4) * P
        nc.scalar.activation(sb(PAR, n0), PS[:, 0, 0:n0], ACT.Copy).then_inc(S("par_act"), 1)
        nc.scalar.activation(sb(PAR + n0, n_par * P - n0), PS[:, 1, 0:n_par * P - n0], ACT.Copy).then_inc(S("par_act"), 1)
        act.wait_ge(S("par_act"), 2)
        act.nop().then_inc(S("par_ready"), 1)
        for k in range(KT):
            b = 2 + k % 2 * 2
            act.wait_ge(S("x_turned"), k + 1)
            nc.scalar.activation(sb(hk(k) + N_META, SEQ), PS[:, b, :], ACT.Copy).then_inc(S("x_taken"), 1)
            nc.scalar.activation(sb(hk(k), N_META), PS[:, b + 1, 0:N_META], ACT.Copy).then_inc(S("x_taken"), 1)
        ln_act(act, hk, hk, T1, lambda k: nc.scalar.activation(
            at(hk(k), T1), at(hk(k), T1), ACT.Identity, bias=pc("ln_in_b", k), scale=pc("ln_in_g", k)))
        take(act, "glu_a", lambda i, acc, j: nc.scalar.activation(
            halves(at(i * AW + (A_ + CONV_K - 1), T1)), acc, ACT.Copy))
        take(act, "glu_g", lambda i, acc, j: nc.scalar.activation(halves(at(i * T1 + B_, T1)), acc, ACT.Sigmoid))
        take(act, "rkv", lambda i, acc, j: nc.scalar.activation(halves(at(i * TP + (R_ + PADT), T1)), acc, ACT.Copy))
        lw = [P, P, 32]
        take(act, "lora", lambda i, acc, j: nc.scalar.activation(
            halves(at(LO + j * LW + 1, T1, 0, lw[j])), acc, ACT.Copy), width=lw)
        act.wait_ge(S("mixed"), 3 * KT + 3)
        nc.scalar.activation(at(LO + 1, T1, 0, HD), at(LO + 1, T1, 0, HD), ACT.Tanh).then_inc(S("lora_act"), 1)
        nc.scalar.activation(at(LO + LW + 1, T1), at(LO + LW + 1, T1), ACT.Sigmoid).then_inc(S("lora_act"), 1)
        nc.scalar.activation(at(LO + 2 * LW + 1, T1, 0, 32), at(LO + 2 * LW + 1, T1, 0, 32), ACT.Sigmoid)\
            .then_inc(S("lora_act"), 1)
        ln_act(act, ck, ck, T1, lambda k: nc.scalar.activation(
            at(ck(k), T1), at(ck(k), T1), ACT.Silu, bias=pc("conv_ln_b", k), scale=pc("conv_ln_g", k)))

        def prep_sig(i):
            if i >= 2:
                act.wait_ge(S("prep_done"), i - 1)
            for n, b, t in (("w0", 0, 0), ("a0", 2, 1)):
                act.wait_ge(S("prep_up"), 2 * i + b // 2 + 1)
                nc.scalar.activation(halves(at(sig[i % 2][t], T1)), PS[:, b:b + 2, 0:C1], ACT.Sigmoid, bias=pc(n, i))\
                    .then_inc(S("prep_sig"), 1)
        prep_sig(0)
        for i in range(KT):
            if i + 1 < KT:
                prep_sig(i + 1)
            if i:
                act.wait_ge(S("prep_done"), i)
            act.wait_ge(S("prep_cum"), i + 1)
            nc.scalar.activation(at(t_[4], T1), at(t_[2], T1), ACT.Exp).then_inc(S("prep_exp"), 1)
            nc.scalar.activation(at(t_[5], T1), at(t_[2], T1), ACT.Exp, scale=-1.0).then_inc(S("prep_exp"), 1)
            nc.scalar.activation(at(t_[3], T1), at(t_[3], T1), ACT.Exp).then_inc(S("prep_exp"), 1)
            act.wait_ge(S("prep_ssm"), i + 1)
            nc.scalar.activation(at(t_[7], T1), at(t_[7], T1), ACT.Sqrt).then_inc(S("prep_sq"), 1)
        bank2 = lambda b: PS[:, b:b + 2, :]
        two_b = lambda ap: ap.rearrange("p (b n) -> p b n", b=2)
        act.nop().then_inc(S("wk_out"), 1)
        act.wait_ge(S("prep_done"), KT)
        act.wait_ge(S("wk_end"), 1)
        with act.Fori(0, NCH) as c:
            for n, off in enumerate((R_, A_)):
                nc.scalar.activation(rav[:, :, n * CH:n * CH + CH], in_chunk(off, c), ACT.Copy).then_inc(S("wk_ra_in"), 1)
            act.wait_ge(S("wk_turned"), c * 2 + 1)
            nc.scalar.activation(two_b(bk), bank2(4), ACT.Copy).then_inc(S("wk_bk"), 1)
            act.wait_ge(S("wk_turned"), c * 2 + 2)
            nc.scalar.activation(two_b(uv)[HD:P], PS[HD:P, 6:8, :], ACT.Copy).then_inc(S("wk_bk"), 1)
            act.wait_ge(S("wk_x0"), c + 1)
            nc.scalar.activation(two_b(sb(W_X, KT * P)), bank2(0), ACT.Copy).then_inc(S("wk_x0_out"), 1)
            for level in range(JOINS):
                for q in range(2):
                    act.wait_ge(S("wk_y"), c * (2 * JOINS) + 2 * level + q + 1)
                    nc.scalar.activation(sb(W_Y + q * BANK, BANK), PS[:, 4 + q, :], ACT.Copy).then_inc(S("wk_y_out"), 1)
            act.wait_ge(S("wk_u"), c + 1)
            nc.scalar.activation(uv[0:HD].rearrange("p (i h v) -> p i h v", h=2, v=HD)[:, :, 0, :],
                                 PS[0:HD, 3, :].rearrange("p (i v) -> p i v", v=HD), ACT.Copy).then_inc(S("wk_u_out"), 1)
            act.wait_ge(S("wk_end"), c + 2)
            act.nop().then_inc(S("wk_end_seen"), 1)
            nc.scalar.activation(in_chunk(R_, c), PS[:, 1, :].rearrange("p (i t) -> p i t", t=CH), ACT.Copy)\
                .then_inc(S("wk_out"), 1)
        take(act, "g_up", lambda i, acc, j: nc.scalar.activation(halves(at(i * T1 + A_, T1)), acc, ACT.Copy))

        def gn_affine(i):
            y = at(R_ + i * TP + PADT, T1)
            act.wait_ge(S("gn_norm"), i + 1)
            nc.scalar.activation(y, y, ACT.Identity, bias=pc("lnx_b", i), scale=pc("lnx_g", i)).then_inc(S("gn_aff"), 1)

        def gn_beside(t):
            i = t // 2
            if t % 2 == 0:
                if i:
                    gn_affine(i - 1)
                act.wait_ge(S("gn_cent"), i + 1)
                if i >= 2:
                    act.wait_ge(S("gn_sum2"), i - 1)
                nc.scalar.activation(at(SQ + i % 2 * T1, T1), at(R_ + i * TP + PADT, T1), ACT.Square).then_inc(S("gn_sq"), 1)
            else:
                act.wait_ge(S("gn_var"), i + 1)
                nc.scalar.activation(at(RSTD, T1), at(RSTD, T1), ACT.Sqrt).then_inc(S("gn_sd"), 1)
        take(act, "gates", lambda i, acc, j: nc.scalar.activation(
            halves(at(i * T1 + K_, T1)), acc, ACT.Sigmoid, bias=at(i + col["b_gate"], 1)), beside=gn_beside)
        gn_affine(KT - 1)
        take(act, "conv_out", lambda i, acc, j: nc.scalar.activation(halves(at(i * T1 + B_, T1)), acc, ACT.Copy))
        take(act, "rwkv_out", lambda i, acc, j: nc.scalar.activation(halves(at(i * T1 + A_, T1)), acc, ACT.Copy),
             pre=[(S("gn_o"), KT)])
        take(act, "w_o", lambda i, acc, j: nc.scalar.activation(halves(at(i * T1 + A_, T1)), acc, ACT.Copy),
             pre=[(S("merged"), KT)])
        affine = lambda n: lambda k: nc.scalar.activation(
            at(hk(k), T1), at(hk(k), T1), ACT.Identity, bias=pc(n + "_b", k), scale=pc(n + "_g", k))
        ln_act(act, hk, hk, T1, affine("ln1"))

        def ffn_free(n):
            if not isinstance(n, int) or n >= 2:
                act.wait_ge(S("ffn_conv"), n * 4 - 4)

        def ffn_silu(n, u):
            act.wait_ge(S("ffn_conv"), n * 4 + 4)
            v = sb(FC + (u * 4 + 2) * T1, 2 * T1)
            nc.scalar.activation(v, v, ACT.Silu).then_inc(S("ffn_silu"), 1)

        def ffn_after(n, u):
            if not isinstance(n, int) or n >= 1:
                ffn_silu(n - 1, 1 - u)
        act.wait_ge(S("ffn_zero"), 1)
        take(act, "ffn_up", lambda i, acc, j: nc.scalar.activation(
            halves(at(UB + j % 8 * UW + FFN_K - 1, T1)), acc, ACT.Copy), free=ffn_free, after=ffn_after)
        ffn_silu(st["ffn_up"].slabs - 1, 0)
        take(act, "ffn_down", lambda i, acc, j: nc.scalar.activation(halves(at(i * T1 + UB, T1)), acc, ACT.Copy),
             pre=[(S("ffn_f"), FT)])
        ln_act(act, hk, hk, T1, lambda k: nc.scalar.activation(
            at(X2 + k * T2 + CTX, SEQ), at(hk(k) + N_META, SEQ), ACT.Identity, bias=pc("ln2_b", k), scale=pc("ln2_g", k)))

    @block.gpsimd
    def _(pool):
        pool.wait_ge(S("x_taken"), 2 * KT)
        pool.wait_ge(S("rows_turned"), 1)
        nc.gpsimd.memset(A[:, R_:R_ + 3 * KT * TP].rearrange("p (i t) -> p i t", t=TP)[:, :, 0:PADT], 0.0)\
            .then_inc(S("mix_zero"), 1)
        nc.gpsimd.memset(A[:, LO:LO + 3 * LW].rearrange("p (i t) -> p i t", t=LW)[:, :, 0:1], 0.0)\
            .then_inc(S("mix_zero"), 1)
        pool.wait_ge(S("mix_zero"), 2)
        pool.wait_ge(S("par_ready"), 1)
        MIXT = TMP + 3 * T1
        for n in range(3 * KT + 3):
            l = n - 3 * KT
            p1 = 32 if l == 2 else P
            off = R_ + n * TP + PADT if l < 0 else LO + l * LW + 1
            pool.wait_ge(*(taken("rkv", n + 1) if l < 0 else taken("lora", l + 1)))
            tmp = at(MIXT + n % 2 * T1, T1, 0, p1)
            if n >= 2:
                pool.wait_ge(S("mixed"), n - 1)
            nc.gpsimd.tensor_tensor(tmp, at(off - 1, T1, 0, p1), at(off, T1, 0, p1), ALU.subtract).then_inc(S("mix_d"), 1)
            pool.wait_ge(S("mix_d"), n + 1)
            mu = pc("mu", n) if l < 2 else pc("mu_last", 0, 32)
            nc.gpsimd.tensor_scalar(tmp, tmp, mu, None, ALU.mult).then_inc(S("mix_mu"), 1)
            pool.wait_ge(S("mix_mu"), n + 1)
            x = at(off, T1, 0, p1)
            nc.gpsimd.tensor_tensor(x, x, tmp, ALU.add).then_inc(S("mixed"), 1)
        pool.wait_ge(S("prep_done"), KT)

        def bk_copies(c):
            for n, off in enumerate((B_, K_)):
                nc.gpsimd.tensor_copy(bk_in[:, :, n * CH:n * CH + CH], in_chunk(off, c)).then_inc(S("wk_bk_in"), 1)

        def v_copy(c):
            pool.wait_ge(S("wk_end"), c + 1)
            nc.gpsimd.tensor_copy(rav[:, :, 2 * CH:3 * CH], in_chunk(V_, c)).then_inc(S("wk_v_in"), 1)
        bk_copies(0)
        v_copy(0)
        with pool.Fori(1, NCH) as c:
            pool.wait_ge(S("wk_scores"), c * 4)
            pool.wait_ge(S("wk_turned"), c * 2)
            bk_copies(c)
            v_copy(c)

    @block.vector
    def _(dve):
        step = Step(dve, S("dve_step"))
        nc.vector.memset(sb(PST, n_par * P), 0.0).then_inc(S("rows_zero"), 1)
        ln_dve(dve, step, hk, hk, T1, LN_EPS)
        step(nc.vector.memset(A[:, A_:A_ + KT * AW].rearrange("p (i t) -> p i t", t=AW)[:, :, 0:CONV_K - 1], 0.0))
        for k in range(KT):
            dve.wait_ge(*taken("glu_g", k + 1))
            x = at(ak(k) + CONV_K - 1, T1)
            nc.vector.tensor_tensor(x, x, at(B_ + k * T1, T1), ALU.mult).then_inc(S("glu"), 1)
        step.done()
        for k in range(KT):
            dve.wait_ge(S("glu"), k + 1)
            nc.vector.tensor_scalar(at(ck(k), T1), at(ak(k), T1), pc("conv_w", k), pc("conv_dw_b", k), ALU.mult, ALU.add)\
                .then_inc(S("conv"), 1)
        with dve.Fori(1, CONV_K) as j:
            for k in range(KT):
                dve.wait_ge(S("conv"), j * KT + (k + 1 - KT))
                nc.vector.scalar_tensor_tensor(
                    out=at(ck(k), T1), in0=at(j + ak(k), T1), scalar=at(j * KT + (col["conv_w"] + k), 1),
                    in1=at(ck(k), T1), op0=ALU.mult, op1=ALU.add).then_inc(S("conv"), 1)
        ln_dve(dve, step, ck, ck, T1, LN_EPS, pre=[(S("conv"), KT * CONV_K)])
        dve.wait_ge(S("mixed"), 3 * KT + 3)
        dve.wait_ge(*ln_done(1))
        step(nc.vector.memset(A[:, A_:A_ + 2 * KT * TP].rearrange("p (i t) -> p i t", t=TP)[:, :, 0:PADT], 0.0))
        V = nc.vector
        T = lambda n: at(t_[n], T1)
        for i in range(KT):
            r, k, v, a, b = (at(o + i * TP + PADT, T1) for o in (R_, K_, V_, A_, B_))
            s0, s1 = (at(o, T1) for o in sig[i % 2])
            k_new = at(kn, T1)
            dve.wait_ge(S("prep_sig"), 2 * i + 1)
            step(V.tensor_scalar(s0, s0, -EXP_HALF, None, ALU.mult))
            step(V.tensor_scalar(T(6), k, pc("k_k", i), None, ALU.mult))
            step.done()
            V.tensor_tensor(T(7), T(6), T(6), ALU.mult).then_inc(S("prep_kk"), 1)
            step(V.tensor_tensor_scan(T(2), at(SCM, T1), s0, 0.0, ALU.mult, ALU.add))
            step.done()
            V.tensor_tensor(T(3), T(2), s0, ALU.subtract).then_inc(S("prep_cum"), 1)
            dve.wait_ge(S("prep_sig"), 2 * i + 2)
            step(V.tensor_scalar(k_new, s1, 1.0, pc("k_a", i), ALU.subtract, ALU.mult))
            step.done()
            step(V.scalar_tensor_tensor(out=k_new, in0=k_new, scalar=1.0, in1=k, op0=ALU.add, op1=ALU.mult))
            step.done()
            dve.wait_ge(S("prep_cum"), i + 1)
            V.scalar_tensor_tensor(out=s0, in0=r, scalar=pc("r_k", i), in1=k_new, op0=ALU.mult, op1=ALU.mult)\
                .then_inc(S("prep_rk"), 1)
            dve.wait_ge(S("prep_ss"), i + 1)
            V.tensor_scalar(halves(T(7)), PS[:, 4:6, 0:C1], 1e-24, None, ALU.max).then_inc(S("prep_ssm"), 1)
            dve.wait_ge(S("prep_exp"), 3 * i + 3)
            step(V.tensor_tensor(k, k_new, T(5), ALU.mult))
            dve.wait_ge(S("prep_rk"), i + 1)
            step(V.tensor_tensor(r, r, T(4), ALU.mult))
            step(V.tensor_copy(at(PL + i * NCH, NCH), A[:, t_[4] + N_META - 1:t_[4] + T1:CH]))
            dve.wait_ge(S("prep_sq"), i + 1)
            step(V.reciprocal(T(7), T(7)))
            step.done()
            step(V.tensor_tensor(T(6), T(6), T(7), ALU.mult))
            step.done()
            step(V.scalar_tensor_tensor(out=a, in0=T(3), scalar=-1.0, in1=T(6), op0=ALU.mult, op1=ALU.mult))
            step(V.tensor_tensor(T(7), T(6), s1, ALU.mult))
            step.done()
            step(V.tensor_tensor(b, T(7), T(5), ALU.mult))
            dve.wait_ge(S("prep_bs"), i + 1)
            step.done()
            V.tensor_tensor(halves(at(BNS + i * T1, T1)), PS[:, 6:8, 0:C1], halves(v), ALU.mult)\
                .then_inc(S("prep_done"), 1)
        dve.wait_ge(S("prep_done"), KT)
        step(V.memset(g_v, 0.0))
        step(V.memset(sb(W_AT, KT * P), 0.0))
        step.done()
        dve.nop().then_inc(S("wk_end"), 1)
        dve.nop().then_inc(S("wk_g"), 1)
        dve.nop().then_inc(S("wk_state"), 1)
        lanes = lambda ap, n: ap.unsqueeze(1).to_broadcast([P, n, P])
        level_mask = lambda level: sb(LVL + level * P, P)
        msv = ms.rearrange("p (h i t) -> p h i t", h=2, t=P)
        uvv = uv.rearrange("p (i h v) -> p i h v", h=2, v=HD)
        with dve.Fori(0, NCH) as c:
            dve.wait_ge(S("wk_end"), c + 1)
            for q in range(4):
                dve.wait_ge(S("wk_scores"), c * 4 + q + 1)
                V.tensor_tensor(ms[:, q * BANK:(q + 1) * BANK].rearrange("p (h t) -> p h t", t=P),
                                PS[:, q, :].rearrange("p (h t) -> p h t", t=P), lanes(sb(MSK, P), 4), ALU.mult)\
                    .then_inc(S("wk_masked"), 1)
            dve.wait_ge(S("wk_masked"), c * 4 + 4)
            for h in range(2):
                V.tensor_copy(at_m[h * HD:(h + 1) * HD, :, h * HD:(h + 1) * HD], msv[0:HD, h, :, CH:2 * CH])\
                    .then_inc(S("wk_at"), 1)
            dve.wait_ge(S("wk_at"), c * 2 + 2)
            V.tensor_tensor(al_m, at_m, lanes(level_mask(0), KT), ALU.mult).then_inc(S("wk_al0"), 1)
            dve.wait_ge(S("wk_al0"), c + 1)
            V.tensor_tensor(xt_m, al_m, lanes(ident, KT), ALU.add).then_inc(S("wk_xt0"), 1)
            dve.wait_ge(S("wk_xt0"), c + 1)
            join_block = lambda level: V.tensor_tensor(
                al_m, at_m, lanes(level_mask(level + 1), KT), ALU.mult).then_inc(S("wk_al"), 1)
            join_block(0)
            for level in range(JOINS):
                if level < JOINS - 1:
                    dve.wait_ge(S("wk_y"), c * (2 * JOINS) + 2 * level + 2)
                    join_block(level + 1)
                if level == 0:
                    dve.wait_ge(S("wk_w"), c + 1)
                    V.tensor_copy(w_v, PS[:, 3, :]).then_inc(S("wk_w3"), 1)
                    dve.wait_ge(S("wk_w3"), c + 1)
                    V.tensor_tensor(w_v, w_v, PS[:, 2, :], ALU.add).then_inc(S("wk_w_out"), 1)
                    dve.wait_ge(S("wk_x0_out"), c + 1)
                for q in range(2):
                    dve.wait_ge(S("wk_join"), c * (2 * JOINS) + 2 * level + q + 1)
                    h = slice(q * BANK, (q + 1) * BANK)
                    if level:
                        dve.wait_ge(S("wk_joined"), c * (4 * JOINS - 2) + 4 * (level - 1) + 2 * q + 2)
                    xt = sb(W_XT, KT * P)[:, h]
                    V.tensor_tensor(xt, xt, PS[:, 6 + q, :], ALU.add).then_inc(S("wk_joined"), 1)
                    if level < JOINS - 1:
                        x = sb(W_X, KT * P)[:, h]
                        V.tensor_tensor(x, x, PS[:, q, :], ALU.add).then_inc(S("wk_joined"), 1)
            dve.wait_ge(S("wk_u"), c + 1)
            V.tensor_copy(uvv[0:HD, :, 1, :], PS[HD:P, 3, :].rearrange("p (i v) -> p i v", v=HD)).then_inc(S("wk_u_out"), 1)
            dve.wait_ge(S("wk_end"), c + 2)
            V.tensor_tensor(g_v, g_v, PS[:, 0, :], ALU.add).then_inc(S("wk_g"), 1)
            dve.wait_ge(S("wk_g"), c + 2)
            gi = g_v.rearrange("p (i v) -> p i v", v=HD)
            last = A[:, PL:PL + KT * NCH].rearrange("p (i c) -> p i c", c=NCH)[:, :, ds(c, 1)]
            V.tensor_tensor(gi, gi, last.to_broadcast([P, KT, HD]), ALU.mult).then_inc(S("wk_state"), 1)
        dve.wait_ge(S("wk_out"), NCH + 1)
        for i in range(KT):
            y = at(R_ + i * TP + PADT, T1)
            rstd = at(RSTD, T1)
            dve.wait_ge(S("gn_sum"), i + 1)
            V.tensor_tensor(halves(y), halves(y), PS[:, 4:6, 0:C1], ALU.subtract).then_inc(S("gn_cent"), 1)
            dve.wait_ge(S("gn_sum2"), i + 1)
            V.tensor_scalar(halves(rstd), PS[:, 6:8, 0:C1], GN_EPS, None, ALU.add).then_inc(S("gn_var"), 1)
            dve.wait_ge(S("gn_sd"), i + 1)
            step(V.reciprocal(rstd, rstd))
            step.done()
            V.tensor_tensor(y, y, rstd, ALU.mult).then_inc(S("gn_norm"), 1)
            dve.wait_ge(S("gn_aff"), i + 1)
            step(V.tensor_tensor(y, y, at(BNS + i * T1, T1), ALU.add))
            step.done()
            dve.wait_ge(*taken("g_up"))
            V.tensor_tensor(y, y, at(A_ + i * T1, T1), ALU.mult).then_inc(S("gn_o"), 1)
        for i in range(KT):
            dve.wait_ge(*taken("conv_out", i + 1))
            y = at(B_ + i * T1, T1)
            step(V.tensor_tensor(y, y, at(K_ + i * T1, T1), ALU.mult))
        for i in range(KT):
            dve.wait_ge(*taken("rwkv_out", i + 1))
            z = at(A_ + i * T1, T1)
            step(V.tensor_tensor(z, z, at(K_ + (KT + i) * T1, T1), ALU.mult))
            step.done()
            y = at(B_ + i * T1, T1)
            V.tensor_tensor(y, y, z, ALU.add).then_inc(S("merged"), 1)
        for i in range(KT):
            dve.wait_ge(*taken("w_o", i + 1))
            V.scalar_tensor_tensor(out=at(hk(i), T1), in0=at(hk(i), T1), scalar=ALPHA, in1=at(A_ + i * T1, T1),
                                   op0=ALU.mult, op1=ALU.add).then_inc(S("res1"), 1)
        V.memset(A[:, UB:UB + 8 * UW].rearrange("p (i t) -> p i t", t=UW)[:, :, 0:FFN_K - 1], 0.0).then_inc(S("ffn_zero"), 1)
        ln_dve(dve, step, hk, hk, T1, LN_EPS, pre=[(S("res1"), KT)])

        s_up = st["ffn_up"]

        def ffn_gate(n, u):
            dve.wait_ge(S("ffn_silu"), n + 1)
            dve.wait_ge(S("ffn_conv"), n * 4 + 4)
            V.tensor_tensor(at(n * (2 * T1) + F_, 2 * T1), sb(FC + u * 4 * T1, 2 * T1), sb(FC + (u * 4 + 2) * T1, 2 * T1),
                            ALU.mult).then_inc(S("ffn_f2"), 1)

        def ffn_one(n, u):
            for tap in range(FFN_K):
                for j in range(4):
                    if tap == 0:
                        dve.wait_ge(S("acc_free"), n * 4 + (FREE0 + s_up.tile0 + j + 1))
                        if j == 0 and (not isinstance(n, int) or n >= 2):
                            dve.wait_ge(S("ffn_f2"), n - 1)
                    else:
                        dve.wait_ge(S("ffn_tap"), n * 8 + 4 * (tap - 1) + j + 1)
                    tile = n * 2 + (j % 2 + j // 2 * FT + tap * 2 * FT + col["ffn_dw"])
                    o, x = at(FC + (u * 4 + j) * T1, T1), at(UB + (u * 4 + j) * UW + tap, T1)
                    if tap == 0:
                        V.tensor_scalar(o, x, at(tile, 1), None, ALU.mult).then_inc(S("ffn_tap"), 1)
                    else:
                        V.scalar_tensor_tensor(out=o, in0=x, scalar=at(tile, 1), in1=o, op0=ALU.mult, op1=ALU.add)\
                            .then_inc(S("ffn_tap" if tap == 1 else "ffn_conv"), 1)
            if not isinstance(n, int) or n >= 1:
                ffn_gate(n - 1, 1 - u)
        loop(dve, s_up.slabs, ffn_one)
        ffn_gate(s_up.slabs - 1, 0)
        dve.wait_ge(S("ffn_f2"), s_up.slabs)
        dve.nop().then_inc(S("ffn_f"), FT)
        for i in range(KT):
            dve.wait_ge(*taken("ffn_down", i + 1))
            V.scalar_tensor_tensor(out=at(hk(i), T1), in0=at(hk(i), T1), scalar=ALPHA, in1=at(UB + i * T1, T1),
                                   op0=ALU.mult, op1=ALU.add).then_inc(S("res2"), 1)
        ln_dve(dve, step, hk, hk, T1, LN_EPS, pre=[(S("res2"), KT)])
        dve_steps[0] = step.n

    block.__exit__(None, None, None)
    shared = ("acc_full", "acc_free", "w_in0", "w_in1", "dve_step")
    over = [n for n in sems if n not in shared and not n.startswith("ln_")]
    nc.clear_and_free_semaphores([sems.pop(n) for n in over])
    nc.all_engine_barrier()
    for l in range(DEPTH2):
        layer(l)
    ctx.close()


_INS = [
    'x', 'meta_tokens', 'ln_in_g', 'ln_in_b', 'w_in', 'b_gate', 'conv_dw', 'conv_dw_b', 'conv_ln_g',
    'conv_ln_b', 'w_conv_out', 'rwkv_mu', 'w0', 'w_decay_up', 'a0', 'a_up', 'g_up', 'k_k', 'k_a', 'r_k',
    'lnx_g', 'lnx_b', 'w_rwkv_out', 'w_o', 'ln1_g', 'ln1_b', 'ffn_up', 'ffn_dw', 'ffn_down', 'ln2_g', 'ln2_b',
    'c_2', 'ctx_2', 'c_ctx_2', 'w_ada_2', 'b_ada_2', 'g_norm1_2', 'g_norm2_2', 'w_in_2', 'na_rpb_2',
    'da_lam_q1_2', 'da_lam_k1_2', 'da_lam_q2_2', 'da_lam_k2_2', 'da_subln_g_2', 'gm_ln_g_2', 'gm_ln_b_2',
    'gm_w_s_2', 'gm_b_s_2', 'w_branch_2', 'w_out_2', 'w_router_2', 'w_e1_2', 'w_e3_2', 'w_e2_2', 'g_final_2',
]


def kernel(**inputs):
    import concourse.bacc as _bacc
    from concourse.bass_utils import run_bass_kernel_spmd as _run

    nc = _bacc.Bacc("TRN2", target_bir_lowering=False, num_devices=1)
    arrays = {name: np.ascontiguousarray(inputs[name]) for name in _INS}
    arrays["const1"], arrays["const2"] = constants_one(), constants_two()
    args = {n: nc.dram_tensor(f"in_{n}", a.shape, F32, kind="ExternalInput").ap() for n, a in arrays.items()}
    result = nc.dram_tensor("out_0", (1, SEQ, D), F32, kind="ExternalOutput").ap()
    build(nc, args, result)
    r = _run(nc, [{f"in_{n}": a for n, a in arrays.items()}], core_ids=[0])
    return r.results[0]["out_0"]
```
